# Optimizing a Trainium2 kernel written in Bass

```python
import math
import jax, jax.numpy as jnp
from jax import lax
import numpy as np

D_MODEL = 2048
BATCH = 1
SEQ = 256
DEPTH = 2

CHUNK = 64
Q_BLOCK = 128
N_A = DEPTH // 2
N_B = DEPTH - N_A
CONV_E = D_MODEL
CONV_WIDTH = 31
DIFF_HEADS = 8
DIFF_HEAD_DIM = 128
DIFF_QK = DIFF_HEADS * 2 * DIFF_HEAD_DIM
DIFF_V = DIFF_HEADS * 2 * DIFF_HEAD_DIM
EPS = 1e-6


def _rms_norm(x, g):
    xf = x.astype(jnp.float32)
    y = xf * lax.rsqrt(jnp.mean(xf * xf, axis=-1, keepdims=True) + EPS)
    return (y * g.astype(jnp.float32)).astype(x.dtype)

def _layer_norm(x, g, b):
    xf = x.astype(jnp.float32)
    mu = jnp.mean(xf, axis=-1, keepdims=True)
    xc = xf - mu
    y = xc * lax.rsqrt(jnp.mean(xc * xc, axis=-1, keepdims=True) + EPS)
    return (y * g.astype(jnp.float32) + b.astype(jnp.float32)).astype(x.dtype)

def _depthwise_causal_conv(y, w, b):
    e = y.shape[-1]
    out = lax.conv_general_dilated(
        y, w.reshape(CONV_WIDTH, 1, e).astype(y.dtype),
        window_strides=(1,), padding=[(CONV_WIDTH - 1, 0)],
        dimension_numbers=("NWC", "WIO", "NWC"), feature_group_count=e)
    return out + b.astype(y.dtype)

def _conformer_layer(x, norm_g, w_in, dw_w, dw_b, ln_g, ln_b, w_out):
    h = _rms_norm(x, norm_g)
    u = h @ w_in
    a, b, z = jnp.split(u, 3, axis=-1)
    y = a * jax.nn.sigmoid(b)
    y = _depthwise_causal_conv(y, dw_w, dw_b)
    y = jax.nn.silu(_layer_norm(y, ln_g, ln_b))
    y = y * jax.nn.silu(z)
    return x + y @ w_out

def _diff_attention(q, k, v, lam):
    bsz, s, h, _, dh = q.shape
    nb = s // Q_BLOCK
    qb = q.reshape(bsz, nb, Q_BLOCK, h, 2, dh).transpose(1, 0, 2, 3, 4, 5)
    key_chunk = jnp.arange(s) // CHUNK

    def block(args):
        q_blk, start = args
        q_chunk = (start + jnp.arange(Q_BLOCK)) // CHUNK
        mask = key_chunk[None, :] <= q_chunk[:, None]
        sc = jnp.einsum("bqhmd,bkhmd->bhmqk", q_blk, k,
                        preferred_element_type=jnp.float32)
        sc = jnp.where(mask, sc, -jnp.inf)
        p = jax.nn.softmax(sc, axis=-1).astype(v.dtype)
        o = jnp.einsum("bhmqk,bkhe->bqhme", p, v)
        return o[:, :, :, 0] - lam * o[:, :, :, 1]

    starts = jnp.arange(nb) * Q_BLOCK
    out = lax.map(block, (qb, starts))
    return out.transpose(1, 0, 2, 3, 4).reshape(bsz, s, h, 2 * dh)

def _diff_layer(x, k, v, norm_g, w_in, q_norm_g, lam_p, subln_g, w_out, layer_idx):
    bsz, s, _ = x.shape
    lam_init = 0.8 - 0.6 * math.exp(-0.3 * (layer_idx - 1))
    h = _rms_norm(x, norm_g)
    u = h @ w_in
    q = u[..., :DIFF_QK].reshape(bsz, s, DIFF_HEADS, 2, DIFF_HEAD_DIM)
    z = u[..., DIFF_QK:]
    q = _rms_norm(q, q_norm_g) * (DIFF_HEAD_DIM ** -0.5)
    lp = lam_p.astype(jnp.float32)
    lam = (jnp.exp(jnp.sum(lp[0] * lp[1])) - jnp.exp(jnp.sum(lp[2] * lp[3]))
           + lam_init).astype(x.dtype)
    o = _diff_attention(q, k, v, lam)
    o = _rms_norm(o, subln_g) * (1.0 - lam_init)
    o = o.reshape(bsz, s, DIFF_V) * jax.nn.silu(z)
    return x + o @ w_out

def first_inputs(seed: int = 0) -> dict:
    key = jax.random.key(seed)
    ks = jax.random.split(key, 20)

    def w(k, shape, fan_in):
        return jax.random.normal(k, shape, jnp.float32) * (fan_in ** -0.5)

    def gain(k, shape):
        return 1.0 + 0.02 * jax.random.normal(k, shape, jnp.float32)

    def bias(k, shape):
        return 0.02 * jax.random.normal(k, shape, jnp.float32)

    return {
        "x": jax.random.normal(ks[0], (BATCH, SEQ, D_MODEL), jnp.float32),
        "a_norm_g": gain(ks[1], (N_A, D_MODEL)),
        "a_w_in": w(ks[2], (N_A, D_MODEL, 3 * CONV_E), D_MODEL),
        "a_dw_w": w(ks[3], (N_A, CONV_WIDTH, CONV_E), CONV_WIDTH),
        "a_dw_b": bias(ks[4], (N_A, CONV_E)),
        "a_ln_g": gain(ks[5], (N_A, CONV_E)),
        "a_ln_b": bias(ks[6], (N_A, CONV_E)),
        "a_w_out": w(ks[7], (N_A, CONV_E, D_MODEL), CONV_E),
        "kv_norm_g": gain(ks[8], (D_MODEL,)),
        "w_kv": w(ks[9], (D_MODEL, DIFF_QK + DIFF_V), D_MODEL),
        "k_norm_g": gain(ks[10], (DIFF_HEAD_DIM,)),
        "b_norm_g": gain(ks[11], (N_B, D_MODEL)),
        "b_w_in": w(ks[12], (N_B, D_MODEL, DIFF_QK + DIFF_V), D_MODEL),
        "b_q_norm_g": gain(ks[13], (N_B, DIFF_HEAD_DIM)),
        "b_lambda": 0.1 * jax.random.normal(ks[14], (N_B, 4, DIFF_HEAD_DIM), jnp.float32),
        "b_subln_g": gain(ks[15], (N_B, 2 * DIFF_HEAD_DIM)),
        "b_w_out": w(ks[16], (N_B, DIFF_V, D_MODEL), DIFF_V),
    }

def first_block(x, a_norm_g, a_w_in, a_dw_w, a_dw_b, a_ln_g, a_ln_b, a_w_out,
              kv_norm_g, w_kv, k_norm_g, b_norm_g, b_w_in, b_q_norm_g,
              b_lambda, b_subln_g, b_w_out):
    bsz, s, _ = x.shape
    k = None
    v = None
    for layer in range(DEPTH):
        if layer < N_A:
            x = _conformer_layer(x, a_norm_g[layer], a_w_in[layer], a_dw_w[layer],
                                 a_dw_b[layer], a_ln_g[layer], a_ln_b[layer],
                                 a_w_out[layer])
        else:
            if layer == N_A:
                kv = _rms_norm(x, kv_norm_g) @ w_kv
                k = _rms_norm(kv[..., :DIFF_QK].reshape(
                    bsz, s, DIFF_HEADS, 2, DIFF_HEAD_DIM), k_norm_g)
                v = kv[..., DIFF_QK:].reshape(bsz, s, DIFF_HEADS, 2 * DIFF_HEAD_DIM)
            j = layer - N_A
            x = _diff_layer(x, k, v, b_norm_g[j], b_w_in[j], b_q_norm_g[j],
                            b_lambda[j], b_subln_g[j], b_w_out[j], layer + 1)
    return x


DEPTH_2 = 1

SB_HEADS = 8
SB_HEAD_DIM = 128
SB_WIDTH = SB_HEADS * SB_HEAD_DIM
MLA_HEADS = 8
MLA_NOPE_DIM = 128
MLA_ROPE_DIM = 64
MLA_QK_DIM = MLA_NOPE_DIM + MLA_ROPE_DIM
MLA_V_DIM = 128
MLA_WIDTH = MLA_HEADS * MLA_V_DIM
Q_LORA_RANK = 512
KV_LORA_RANK = 256
ROPE_THETA = 10000.0
D_MIX = SB_WIDTH + MLA_WIDTH
IN_SPLITS = (SB_WIDTH, SB_WIDTH, SB_WIDTH, SB_WIDTH,
             Q_LORA_RANK, KV_LORA_RANK, MLA_ROPE_DIM, MLA_WIDTH)
D_IN = sum(IN_SPLITS)


def rms_norm(x, w):
    xf = x.astype(jnp.float32)
    y = xf * lax.rsqrt(jnp.mean(xf * xf, axis=-1, keepdims=True) + EPS)
    return (y * w.astype(jnp.float32)).astype(x.dtype)

def rope_tables(positions):
    inv_freq = ROPE_THETA ** (-jnp.arange(0, MLA_ROPE_DIM, 2, dtype=jnp.float32) / MLA_ROPE_DIM)
    ang = positions.astype(jnp.float32)[..., None] * inv_freq
    return jnp.cos(ang), jnp.sin(ang)

def apply_rope(x, cos, sin):
    x1, x2 = jnp.split(x.astype(jnp.float32), 2, axis=-1)
    out = jnp.concatenate([x1 * cos - x2 * sin, x2 * cos + x1 * sin], axis=-1)
    return out.astype(x.dtype)

def to_heads(t, n_heads):
    b, s, _ = t.shape
    return t.reshape(b, s, n_heads, -1).transpose(0, 2, 1, 3)

def from_heads(t):
    b, h, s, d = t.shape
    return t.transpose(0, 2, 1, 3).reshape(b, s, h * d)

def stick_breaking_attention(q, k, v):
    seq, d = q.shape[2], q.shape[3]
    scale = 1.0 / math.sqrt(d)
    outs = []
    for b0 in range(0, seq, Q_BLOCK):
        kl = b0 + Q_BLOCK
        z = jnp.einsum('bhqd,bhkd->bhqk', q[:, :, b0:kl], k[:, :, :kl]).astype(jnp.float32) * scale
        t_idx = b0 + jnp.arange(Q_BLOCK)[:, None]
        s_idx = jnp.arange(kl)[None, :]
        before = s_idx < t_idx
        log_keep = jnp.where(before, jax.nn.log_sigmoid(-z), 0.0)
        later = lax.cumsum(log_keep, axis=3, reverse=True) - log_keep
        a = jnp.where(before, jnp.exp(jax.nn.log_sigmoid(z) + later), 0.0)
        outs.append(jnp.einsum('bhqk,bhkd->bhqd', a.astype(v.dtype), v[:, :, :kl]))
    return jnp.concatenate(outs, axis=2)

def chunk_causal_softmax_attention(q, k, v):
    seq, d = q.shape[2], q.shape[3]
    scale = 1.0 / math.sqrt(d)
    outs = []
    for b0 in range(0, seq, Q_BLOCK):
        kl = b0 + Q_BLOCK
        s_ = jnp.einsum('bhqd,bhkd->bhqk', q[:, :, b0:kl], k[:, :, :kl]).astype(jnp.float32) * scale
        t_chunk = (b0 + jnp.arange(Q_BLOCK))[:, None] // CHUNK
        s_chunk = jnp.arange(kl)[None, :] // CHUNK
        s_ = jnp.where(s_chunk <= t_chunk, s_, -jnp.inf)
        p = jax.nn.softmax(s_, axis=-1)
        outs.append(jnp.einsum('bhqk,bhkd->bhqd', p.astype(v.dtype), v[:, :, :kl]))
    return jnp.concatenate(outs, axis=2)

def hybrid_layer(x, cos, sin, pre_norm_w, w_in, q_norm_w, w_q_up, kv_norm_w, w_kv_up, w_out, post_norm_w):
    b, s, _ = x.shape
    h = rms_norm(x, pre_norm_w)
    proj = h @ w_in
    split_pts = tuple(int(i) for i in np.cumsum(IN_SPLITS)[:-1])
    sb_q, sb_k, sb_v, sb_gate, c_q, c_kv, k_rope, mla_gate = jnp.split(proj, split_pts, axis=-1)

    o_a = from_heads(stick_breaking_attention(to_heads(sb_q, SB_HEADS),
                                              to_heads(sb_k, SB_HEADS),
                                              to_heads(sb_v, SB_HEADS)))

    q_full = (rms_norm(c_q, q_norm_w) @ w_q_up).reshape(b, s, MLA_HEADS, MLA_QK_DIM)
    q_nope, q_rot = jnp.split(q_full, [MLA_NOPE_DIM], axis=-1)
    q_rot = apply_rope(q_rot, cos[:, :, None, :], sin[:, :, None, :])
    kv = (rms_norm(c_kv, kv_norm_w) @ w_kv_up).reshape(b, s, MLA_HEADS, MLA_NOPE_DIM + MLA_V_DIM)
    k_nope, v_mla = jnp.split(kv, [MLA_NOPE_DIM], axis=-1)
    k_rot = apply_rope(k_rope, cos, sin)
    k_rot = jnp.broadcast_to(k_rot[:, :, None, :], (b, s, MLA_HEADS, MLA_ROPE_DIM))
    q_mla = jnp.concatenate([q_nope, q_rot], axis=-1).transpose(0, 2, 1, 3)
    k_mla = jnp.concatenate([k_nope, k_rot], axis=-1).transpose(0, 2, 1, 3)
    o_b = from_heads(chunk_causal_softmax_attention(q_mla, k_mla, v_mla.transpose(0, 2, 1, 3)))

    mixed = jnp.concatenate([o_a * jax.nn.silu(sb_gate), o_b * jax.nn.silu(mla_gate)], axis=-1)
    y = mixed @ w_out
    return x + rms_norm(y, post_norm_w)

def second_inputs(seed: int = 0) -> dict:
    key = jax.random.key(seed)
    ks = jax.random.split(key, 12)
    f32 = jnp.float32
    x = jax.random.normal(ks[0], (BATCH, SEQ, D_MODEL), f32)
    positions = jnp.broadcast_to(jnp.arange(SEQ, dtype=jnp.int32)[None, :], (BATCH, SEQ))
    pre_norm_w = 1.0 + 0.05 * jax.random.normal(ks[1], (DEPTH_2, D_MODEL), f32)
    w_in = jax.random.normal(ks[2], (DEPTH_2, D_MODEL, D_IN), f32) * D_MODEL ** -0.5
    q_norm_w = 1.0 + 0.05 * jax.random.normal(ks[3], (DEPTH_2, Q_LORA_RANK), f32)
    w_q_up = jax.random.normal(ks[4], (DEPTH_2, Q_LORA_RANK, MLA_HEADS * MLA_QK_DIM), f32) * Q_LORA_RANK ** -0.5
    kv_norm_w = 1.0 + 0.05 * jax.random.normal(ks[5], (DEPTH_2, KV_LORA_RANK), f32)
    w_kv_up = jax.random.normal(ks[6], (DEPTH_2, KV_LORA_RANK, MLA_HEADS * (MLA_NOPE_DIM + MLA_V_DIM)), f32) * KV_LORA_RANK ** -0.5
    w_out = jax.random.normal(ks[7], (DEPTH_2, D_MIX, D_MODEL), f32) * D_MIX ** -0.5
    post_norm_w = 1.0 + 0.05 * jax.random.normal(ks[8], (DEPTH_2, D_MODEL), f32)
    return {'x': x, 'positions': positions, 'pre_norm_w': pre_norm_w, 'w_in': w_in,
            'q_norm_w': q_norm_w, 'w_q_up': w_q_up, 'kv_norm_w': kv_norm_w, 'w_kv_up': w_kv_up,
            'w_out': w_out, 'post_norm_w': post_norm_w}

def second_block(x, positions, pre_norm_w, w_in, q_norm_w, w_q_up, kv_norm_w, w_kv_up, w_out, post_norm_w):
    cos, sin = rope_tables(positions)
    for i in range(DEPTH_2):
        x = hybrid_layer(x, cos, sin, pre_norm_w[i], w_in[i], q_norm_w[i], w_q_up[i],
                         kv_norm_w[i], w_kv_up[i], w_out[i], post_norm_w[i])
    return x


def setup_inputs(seed=0):
    out = dict(first_inputs(seed))
    for name, value in second_inputs(seed + 1).items():
        if name != "x":
            out[name + "_2"] = value
    return out


def reference(
    x, a_norm_g, a_w_in, a_dw_w, a_dw_b, a_ln_g, a_ln_b, a_w_out, kv_norm_g, w_kv, k_norm_g,
    b_norm_g, b_w_in, b_q_norm_g, b_lambda, b_subln_g, b_w_out, positions_2, pre_norm_w_2,
    w_in_2, q_norm_w_2, w_q_up_2, kv_norm_w_2, w_kv_up_2, w_out_2, post_norm_w_2,
):
    x = first_block(
        x, a_norm_g, a_w_in, a_dw_w, a_dw_b, a_ln_g, a_ln_b, a_w_out, kv_norm_g, w_kv, k_norm_g,
        b_norm_g, b_w_in, b_q_norm_g, b_lambda, b_subln_g, b_w_out,
    )
    return second_block(
        x, positions_2, pre_norm_w_2, w_in_2, q_norm_w_2, w_q_up_2, kv_norm_w_2, w_kv_up_2,
        w_out_2, post_norm_w_2,
    )


_drawn_inputs = setup_inputs


def setup_inputs(seed=0):
    import zlib

    import numpy as np

    out = dict(_drawn_inputs(seed))
    spreads = {}
    factors = {'a_norm_g': 3.519,
     'a_ln_g': 4.238,
     'a_ln_b': 4.827,
     'kv_norm_g': 4.303,
     'k_norm_g': 5.376,
     'b_norm_g': 4.44,
     'b_q_norm_g': 5.962,
     'b_lambda': 4.225,
     'b_subln_g': 21.717,
     'q_norm_w_2': 30.462,
     'kv_norm_w_2': 19.667,
     'pre_norm_w_2': 2.962,
     'post_norm_w_2': 49.4}
    for name, (base, spread) in spreads.items():
        noise = np.random.default_rng([zlib.crc32(name.encode()), seed]).standard_normal(out[name].shape)
        drawn = base * np.exp(spread * noise) if base else spread * noise
        out[name] = __import__('jax').numpy.asarray(drawn.astype(out[name].dtype))
    for name, factor in factors.items():
        out[name] = (out[name] * factor).astype(out[name].dtype)
    return out
```

```python
import math

import numpy as np

import concourse.bass as bass
from concourse import mybir
from contextlib import ExitStack

F32 = mybir.dt.float32
F32R = mybir.dt.float32r
ACT = mybir.ActivationFunctionType
ALU = mybir.AluOpType
AX = mybir.AxisListType

P = 128
SEQ = 256
TT = SEQ // P
D = 2048
KT = D // P
NC = 512
TAPS = 31
PAD = TAPS - 1
EPS = 1e-6
DH = 128
ROT = 64
HEADS = 8
LAM_INIT = 0.8 - 0.6 * math.exp(-0.3 * (2 - 1))
MASKED = -1e30
ROPE_THETA = 10000.0

UP = list(range(KT))
CHUNKS = []
for j in range(4):
    CHUNKS += [("a_w_in", j * NC, NC, UP, "A", 0), ("a_w_in", D + j * NC, NC, UP, "A", 0)]
CHUNKS += [("a_w_in", 2 * D + j * NC, NC, UP, "A", 0) for j in range(4)]
CHUNKS += [("a_w_out", j * NC, NC, UP, "B", 0) for j in range(4)]
CHUNKS += [("w_kv", j * NC, NC, UP, "A", 0) for j in range(8)]
CHUNKS += [("b_w_in", j * NC, NC, UP, "B", 0) for j in range(8)]
CHUNKS += [("b_w_out", j * NC, NC, UP, "A", 0) for j in range(4)]
IN2 = dict(sb_q=0, sb_k=1024, sb_v=2048, sb_gate=3072, c_q=4096, c_kv=4608, mla_gate=4928)
CHUNKS += [("w_in_2", IN2["c_q"], 512, UP, "B", 0), ("w_in_2", IN2["c_kv"], 320, UP, "B", 0)]
CHUNKS += [("w_q_up_2", j * 384, 384, UP[:4], "A", 0) for j in range(4)]
CHUNKS += [("w_kv_up_2", j * NC, NC, UP[:2], "A", 4) for j in range(4)]
for part in ("sb_q", "sb_k", "sb_v", "mla_gate", "sb_gate"):
    CHUNKS += [("w_in_2", IN2[part] + j * NC, NC, UP, "B", 0) for j in range(2)]
CHUNKS += [("w_out_2", j * NC, NC, UP[8:] + UP[:8], "A", 0) for j in range(4)]
C_Z, C_OUT, C_K, C_V, C_Q, C_ZB, C_OUTB = 8, 12, 16, 20, 24, 28, 32
C_CQ, C_CKV, C_QUP, C_KVUP, C_SBQ, C_SBK, C_SBV, C_MG, C_SG, C_OUT2 = 36, 37, 38, 42, 46, 48, 50, 52, 54, 56
NCH = len(CHUNKS)

UNITS = [(c, i) for c in range(NCH) for i in range(len(CHUNKS[c][3]) // 2)]
FIRST = [next(u for u, (c, _) in enumerate(UNITS) if c == n) for n in range(NCH)] + [len(UNITS)]
NU = len(UNITS)
CONV_FROM = [19, 35, 51, 67]
CONV_RATE = 9
CONV_SLOTS = -(-4 * TAPS // CONV_RATE)
WHOLE = [any(f + AHEAD <= u < f + CONV_SLOTS + AHEAD for f in CONV_FROM) for AHEAD in (2,) for u in range(NU)]
SPLITS = []
SPLIT_NO = {}
for u in range(NU):
    if not WHOLE[u]:
        SPLIT_NO[u] = len(SPLITS)
        SPLITS.append(u)
RAW, PARTS = 4, 3
AHEAD = PARTS - 1

DIFF_FROM, DIFF_STEP = FIRST[C_ZB] - 8, 5
MLA_FROM, MLA_STEP = FIRST[C_SBQ] + 3, 5
SB_FROM, SB_STEP = FIRST[C_MG], 4
GATE_AT = [FIRST[C_ZB + 1], FIRST[C_ZB + 2], FIRST[C_ZB + 3], FIRST[C_OUTB] + 2]
OG_AT = [GATE_AT[0] + 2, GATE_AT[1] + 2, GATE_AT[2] + 2, GATE_AT[3] + 1]

T_EVENTS = [(f"x{j}", "lo") for j in range(4)] + [(f"y{j}", "copy") for j in range(4)]
T_EVENTS += [(f"z{j}", "mul") for j in range(4)] + [(f"w{j}", "lo") for j in range(4)] + [("b0", "lo")]
for j in range(3):
    T_EVENTS += [(f"k{j}", "copy"), (f"b{j + 1}", "lo")]
T_EVENTS += [("k3", "copy")] + [(f"q{j}", "copy") for j in range(4)] + [(f"og{j}", "mul0") for j in range(4)]
T_EVENTS += [(f"v{j}", "lo") for j in range(4)] + [("cq", "lo"), ("ckv", "lo")]
T_EVENTS += [(f"qu{j}", "copy") for j in range(4)] + [(f"ku{j}", "copy") for j in range(4)]
T_EVENTS += [(f"sq{j}", "copy") for j in range(2)] + [(f"sk{j}", "copy") for j in range(2)]
T_EVENTS += [(f"mg{j}", "mul") for j in range(2)] + [(f"sg{j}", "mul") for j in range(2)]
T_EVENTS = [(n, "lo" if k == "mul0" else k) for n, k in T_EVENTS]
T_NO = {n: i for i, (n, _) in enumerate(T_EVENTS)}
LO_NO = {n: i for i, n in enumerate([n for n, k in T_EVENTS if k != "copy"])}
MUL_NO = {n: i for i, n in enumerate([n for n, k in T_EVENTS if k == "mul"])}
COPY_NO = {n: i for i, n in enumerate([n for n, k in T_EVENTS if k == "copy"])}

RS = [("x", 2), ("ln", 2), ("x1", 2)] + [(f"k{j}", 8) for j in range(4)] + [(f"q{j}", 8) for j in range(3)]
RS += [("o0", 2), ("q3", 8)] + [(f"o{h}", 2) for h in range(1, HEADS)] + [("x2", 2), ("cq", 2), ("ckv", 2), ("post", 2)]
RS_NO = {n: i for i, (n, _) in enumerate(RS)}
SS_NO = {n: i for i, n in enumerate([n for n, _ in RS if n != "ln"])}

BY_DVE = set(range(C_OUT, C_V)) | set(range(C_Q, C_ZB)) | set(range(C_OUTB, C_CQ)) | set(range(C_OUT2, NCH))

ROWS = {}
for name, n in (("a_norm_g", 16), ("a_ln_g", 16), ("a_ln_b", 16), ("a_dw_b", 16), ("kv_norm_g", 16),
                ("b_norm_g", 16), ("pre_norm_w_2", 16), ("k_norm_g", 1), ("b_q_norm_g", 1),
                ("b_subln_g", 2), ("q_norm_w_2", 4), ("kv_norm_w_2", 2)):
    ROWS[name] = (sum(k for _, k in ROWS.values()), n)
NROWS = sum(k for _, k in ROWS.values())

PI_A = 6.28125
PI_B = float(np.float32(np.round((2 * math.pi - PI_A) * 2 ** 20) / 2 ** 20))
PI_C = 2 * math.pi - PI_A - PI_B
ROUND = 12582912.0
PI_LOW = 3.1415925

SEMS = """x0_loaded x1_loaded x2_loaded x3_loaded rows_loaded post_gain_loaded out_stored
w0_loaded w1_loaded w2_loaded w3_loaded consts_ready
units_done t_full tables_full
w_hi_ready t_hi_ready t_copied chunk_read_act sumsq_ready guess_ready act_chain
w_lo_ready t_multiplied lo_ready chunk_read_dve var_ready dve_chain
tables_ready x_scale_ready sig_ready y_ready conv_ready stats_full stats_read diag_ready
moments_full moments_ready normed silu_ready zt_hi x1_ready x1_scale_ready x2_ready x2_scale_ready
lam_in lam_exp angle_ready sines_ready rope_ready
k_ready q_ready vals_ready gate_read zs_ready on_ready
d_scores d_negmax d_exp d_probs d_pt d_pt_copied d_out d_gated
cq_scale ckv_scale kr_staged kr_roped qu_staged qu_roped ku_staged sb_staged
m_scores m_negmax m_exp m_probs m_pt m_pt_copied m_out m_out_copied
s_scores s_soft s_keep s_later s_logit s_weight s_masked s_out s_out_copied
y_scaled y_squared final_scale final_ready""".split()


def hybrid_program(nc, t, out):
    with ExitStack() as ctx:
        def sb(name, shape, dt=F32):
            return ctx.enter_context(nc.sbuf_tensor(name, shape, dt))

        S = {n: ctx.enter_context(nc.semaphore(n)) for n in SEMS}

        x_res = sb("x_res", [P, TT, D])
        hi = {"A": sb("actA_hi", [P, KT, SEQ], F32R), "B": sb("actB_hi", [P, KT, SEQ], F32R)}
        lo = {"A": sb("actA_lo", [P, KT, SEQ], F32R), "B": sb("actB_lo", [P, KT, SEQ], F32R)}
        w_raw = sb("w_raw", [P, RAW, 2 * NC])
        w_hi = sb("w_hi", [P, PARTS, 2 * NC], F32R)
        w_lo = sb("w_lo", [P, PARTS, 2 * NC], F32R)
        stage = sb("stage", [P, 2, TT, NC])
        heads_out = sb("heads_out", [P, 4, TT, 2 * DH])
        work = sb("work", [P, 2, 384])
        probs_t = sb("probs_t", [P, 384])
        ident = sb("ident", [P, P])
        strict = sb("strict", [P, P])
        after = sb("after", [P, P])
        ones = sb("ones", [P, P])
        neg_ones = sb("neg_ones", [P, P])
        mask_row = sb("mask_row", [1, P + 64])
        gains = sb("gains", [P, NROWS + 6])
        st = sb("st", [P, 1024])
        rope = sb("rope", [P, 8, TT, 32])
        pos_i = sb("pos_i", [P, TT], mybir.dt.int32)
        aux = sb("aux", [P, 14592])
        PS = ctx.enter_context(nc.psum_tensor("PS", [P, 8, NC], F32))

        def view(at, *shape):
            n = int(np.prod(shape))
            a = aux[:, at:at + n]
            if len(shape) == 3:
                return a.rearrange("p (a b c) -> p a b c", a=shape[0], b=shape[1])
            return a.rearrange("p (a b) -> p a b", a=shape[0]) if len(shape) == 2 else a

        y_pad = view(0, KT, PAD + SEQ)
        conv = view(KT * (PAD + SEQ), KT, SEQ)
        x_t = view(KT * (PAD + 2 * SEQ), KT, SEQ)
        taps = view(KT * (PAD + 3 * SEQ), KT, TAPS)
        moments = view(KT * (PAD + 3 * SEQ + TAPS), 2, SEQ)
        diag = view(KT * (PAD + 3 * SEQ + TAPS) + 2 * SEQ, 4, P)
        k_t = view(0, KT, SEQ)
        q_t = view(KT * SEQ, KT, SEQ)
        vals = view(2 * KT * SEQ, TT, D)
        H8 = HEADS * SEQ
        qn_t, kn_t, qr_t = view(0, HEADS, SEQ), view(H8, HEADS, SEQ), view(2 * H8, HEADS, SEQ)
        v_mla, sq_t, sk_t = view(3 * H8, TT, HEADS * DH), view(4 * H8, HEADS, SEQ), view(5 * H8, HEADS, SEQ)
        v_sb, kr_t = view(6 * H8, TT, HEADS * DH), view(7 * H8, SEQ)
        yw = view(0, TT, D)
        post_gain = aux[:, 2 * H8:3 * H8]
        qu_stage = heads_out[:, :, :, :].rearrange("p a b c -> p (a b c)")[:, 0:4 * 384]\
            .rearrange("p (i t n) -> p i t n", i=2, t=TT)
        junk = heads_out[:, :, :, :].rearrange("p a b c -> p (a b c)")

        cursor = [0]

        def small(n):
            cursor[0] += n
            return st[:, cursor[0] - n:cursor[0]]

        root = {n: dict(ss=small(k), v=small(k), ln=small(k), y=small(k), t=small(k), r=small(k))
                for n, k in RS}
        k_scale = {f"{m}{j}": small(8) for m in "kq" for j in range(4)}
        cq_scale, ckv_scale = small(2), small(2)
        qk_gain, sub_gain = small(1), small(2)
        lam_sums, lam_exps, neg_lam = small(2), small(2), small(1)
        bn = small(2 * 4 * 6)
        mv = small(4)
        y_sums = small(8)
        neg_max, sums, recips, neg_r = small(4), small(4), small(4), small(2)
        pos_f = small(2)

        def gain(name, i):
            r, _ = ROWS[name]
            return gains[:, r + i:r + i + 1]

        def act_hi(which, k):
            return hi[which][:, k, :]

        def chunk_bank(c, tok, w=None):
            return PS[:, 2 * (c % 2) + tok, 0:(w or CHUNKS[c][2])]

        def w_view(ring, slot, w):
            return ring[:, slot, 0:2 * w].rearrange("p (k n) -> p k n", k=2)

        def bank_pair(i):
            return PS[:, 4 + i, :].rearrange("p (c s) -> p c s", c=2)

        def chunk_done(eng, c):
            eng.wait_ge(S["units_done"], FIRST[c + 1])

        def transposed(eng, name):
            eng.wait_ge(S["t_full"], T_NO[name] + 1)

        block = ctx.enter_context(nc.Block())

        @block.sync
        def _(sp):
            for j in range(4):
                sp.dma_start(x_res[:, :, j * NC:(j + 1) * NC],
                             t["x"][0, :, j * NC:(j + 1) * NC].rearrange("(t p) n -> p t n", p=P))\
                    .then_inc(S[f"x{j}_loaded"], 16)
            for u, (c, i) in enumerate(UNITS):
                name, col, w, kts, _, _ = CHUNKS[c]
                if u >= RAW:
                    if WHOLE[u - RAW]:
                        sp.wait_ge(S["units_done"], u - RAW + 1)
                    else:
                        sp.wait_ge(S["w_lo_ready"], SPLIT_NO[u - RAW] + 1)
                k = kts[2 * i]
                sp.dma_start(w_view(w_raw, u % RAW, w),
                             t[name].rearrange("o (k p) n -> (o k) p n", p=P)[k:k + 2, :, col:col + w]
                             .rearrange("k p n -> p k n")).then_inc(S[f"w{u % RAW}_loaded"], 16)
                if u == FIRST[C_SG]:
                    sp.wait_ge(S["m_out"], HEADS)
                    sp.dma_start(post_gain, t["post_norm_w_2"][0:1, :].to_broadcast([P, D]))\
                        .then_inc(S["post_gain_loaded"], 16)
            for i in range(8):
                sp.wait_ge(S["final_ready"], i + 1)
                tok, j = i % 2, i // 2
                sp.dma_start(out[0, tok * P:(tok + 1) * P, j * NC:(j + 1) * NC],
                             yw[:, tok, j * NC:(j + 1) * NC]).then_inc(S["out_stored"], 16)
            sp.wait_ge(S["out_stored"], 8 * 16)

        @block.gpsimd
        def _(pool):
            chain = nc.gpsimd
            chain.memset(ident[:, :], 0.0)
            chain.memset(strict[:, :], 1.0)
            chain.memset(after[:, :], -1.0)
            chain.memset(ones[:, :], 1.0)
            chain.memset(neg_ones[:, :], -1.0)
            chain.memset(mask_row[:, 64:P], 0.0)
            chain.memset(mask_row[:, 0:64], 1.0)
            chain.memset(mask_row[:, P:P + 64], MASKED)
            chain.memset(y_pad[:, :, 0:PAD], 0.0)
            inv_freq = np.float32(ROPE_THETA) ** (-np.arange(0, ROT, 2, dtype=np.float32) / np.float32(ROT))
            for i in range(ROT // 2):
                last = chain.memset(rope[:, 7, 0, i:i + 1], float(inv_freq[i]))
            last.then_inc(S["consts_ready"], 1)
            pool.wait_ge(S["consts_ready"], 1)
            chain.affine_select(out=ident[:, :], in_=ident[:, :], compare_op=ALU.not_equal, fill=1.0,
                                base=0, pattern=[[-1, P]], channel_multiplier=1)
            chain.affine_select(out=strict[:, :], in_=strict[:, :], compare_op=ALU.is_gt, fill=0.0,
                                base=0, pattern=[[1, P]], channel_multiplier=-1)
            chain.affine_select(out=after[:, :], in_=after[:, :], compare_op=ALU.is_gt, fill=0.0,
                                base=0, pattern=[[-1, P]], channel_multiplier=1).then_inc(S["consts_ready"], 1)

        @block.scalar
        def _(act):
            n_chain = [0]

            def link(ins):
                n_chain[0] += 1
                ins.then_inc(S["act_chain"], 1)
                act.wait_ge(S["act_chain"], n_chain[0])

            EXP_LN, SILU, SIGMOID = "natural_log_exp_and_others", "silu_and_others", "sigmoid_and_others"
            table = [None]

            def want(name):
                if table[0] != name:
                    nc.scalar.preload_act_table_set(name)
                    table[0] = name

            n_rows = [0]

            def load_rows(dst, src):
                n_rows[0] += 16
                act.dma_start(dst, src).then_inc(S["rows_loaded"], 16)

            for name, (r, n) in ROWS.items():
                src = t[name]
                src = src[0, :] if len(src.shape) == 2 else src
                load_rows(stage[r:r + n, 0, 0, 0:P], src.rearrange("(r c) -> r c", c=P))
            load_rows(junk[0:TAPS, 0:D], t["a_dw_w"][0, :, :])
            load_rows(work[:, :, :].rearrange("p a b -> p (a b)")[:, 0:4 * DH],
                      t["b_lambda"].rearrange("o a d -> o (a d)").to_broadcast([P, 4 * DH]))
            with nc.allow_non_contiguous_dma(reason="256 positions, one to a partition and token tile"):
                load_rows(pos_i[:, :], t["positions_2"][0, :].rearrange("(t p) -> p t", p=P))
            assert n_rows[0] == 16 * 15

            act.wait_ge(S["tables_full"], 1)
            nc.scalar.activation(gains[:, 0:NROWS], PS[:, 6, 0:NROWS], ACT.Copy)
            nc.scalar.activation(taps.rearrange("p a b -> p (a b)"), PS[:, 7, 0:KT * TAPS], ACT.Copy)\
                .then_inc(S["tables_ready"], 1)
            act.wait_ge(S["tables_ready"], 1)

            def split(u):
                if u >= NU or WHOLE[u]:
                    return
                n, w = SPLIT_NO[u], CHUNKS[UNITS[u][0]][2]
                act.wait_ge(S[f"w{u % RAW}_loaded"], 16 * (u // RAW + 1))
                if n >= PARTS:
                    act.wait_ge(S["units_done"], SPLITS[n - PARTS] + 1)
                nc.scalar.activation(w_hi[:, n % PARTS, 0:2 * w], w_raw[:, u % RAW, 0:2 * w], ACT.Copy)\
                    .then_inc(S["w_hi_ready"], 1)

            def hi_parts(name, which, k0, gain_name, n=4, g0=None):
                transposed(act, name)
                for i in range(n):
                    g = gain(gain_name, (k0 if g0 is None else g0) + i)
                    ins = nc.scalar.activation(act_hi(which, k0 + i), bank_pair(i // 2)[:, i % 2, :],
                                               ACT.Copy, scale=g)
                    if i % 2:
                        ins.then_inc(S["t_hi_ready"], 1)

            def guess(name):
                want(EXP_LN)
                act.wait_ge(S["var_ready"], RS_NO[name] + 1)
                link(nc.scalar.activation(root[name]["ln"], root[name]["v"], ACT.Ln))
                nc.scalar.activation(root[name]["y"], root[name]["ln"], ACT.Exp, scale=-0.5)\
                    .then_inc(S["guess_ready"], 1)

            def squares_of_rows(name):
                for tok in range(TT):
                    ins = nc.scalar.activation(junk, x_res[:, tok, :], ACT.Square,
                                               accum_out=root[name]["ss"][:, tok:tok + 1])
                    if tok == 0:
                        link(ins)
                ins.then_inc(S["sumsq_ready"], 1)

            def squares_of_chunk(c, w, name, scale):
                for tok in range(TT):
                    ins = nc.scalar.activation(work[:, :, :].rearrange("p a b -> p (a b)")[:, 0:w],
                                               chunk_bank(c, tok, w), ACT.Square,
                                               scale=scale[:, tok:tok + 1],
                                               accum_out=root[name]["ss"][:, tok:tok + 1])
                    if tok == 0:
                        link(ins)
                ins.then_inc(S["sumsq_ready"], 1)

            def evacuate(c, dst, func, scale, w=None, last=True):
                if func != ACT.Copy:
                    want(SILU if func == ACT.Silu else SIGMOID)
                chunk_done(act, c)
                for tok in range(TT):
                    ins = nc.scalar.activation(dst(tok), chunk_bank(c, tok, w), func,
                                               scale=scale[:, tok:tok + 1])
                if last:
                    ins.then_inc(S["chunk_read_act"], 1)
                return ins

            def copy_pairs(name, dst, scale, n=2):
                transposed(act, name)
                for i in range(n):
                    ins = nc.scalar.activation(dst(i), bank_pair(i), ACT.Copy, scale=scale)
                ins.then_inc(S["t_copied"], 1)

            def stage_at(i):
                return lambda tok: stage[:, i, tok, :]

            r_x, r_x1, r_x2 = root["x"]["r"], root["x1"]["r"], root["x2"]["r"]

            for j in range(4):
                transposed(act, f"x{j}")
                for i in range(4):
                    ins = nc.scalar.activation(act_hi("A", 4 * j + i), bank_pair(i // 2)[:, i % 2, :],
                                               ACT.Copy, scale=gain("a_norm_g", 4 * j + i))
                    if i % 2:
                        ins.then_inc(S["t_hi_ready"], 1)
                if j < AHEAD:
                    split(j)
            for j in range(4):
                act.wait_ge(S[f"x{j}_loaded"], 16)
            squares_of_rows("x")
            guess("x")
            act.wait_ge(S["lam_in"], 1)
            nc.scalar.activation(lam_exps, lam_sums, ACT.Exp).then_inc(S["lam_exp"], 1)
            act.wait_ge(S["angle_ready"], 1)
            nc.scalar.activation(rope[:, 2, :, :], rope[:, 0, :, :], ACT.Sin)
            nc.scalar.activation(rope[:, 3, :, :], rope[:, 0, :, :], ACT.Sin, scale=0.5)\
                .then_inc(S["sines_ready"], 1)
            table[0] = "sines"

            for u, (c, s) in enumerate(UNITS):
                if s == 0 and 1 <= c <= C_Z and c % 2:
                    j = c // 2
                    act.wait_ge(S["x_scale_ready"], 1)
                    if j:
                        act.wait_ge(S["y_ready"], j)
                    evacuate(c - 1, stage_at(0), ACT.Copy, r_x)
                if s == 0 and 1 <= c <= C_Z and c % 2 == 0:
                    j = c // 2 - 1
                    if j:
                        transposed(act, f"y{j - 1}")
                    ins = evacuate(c - 1, stage_at(1), ACT.Sigmoid, r_x, last=False)
                    ins.then_inc(S["sig_ready"], 1)
                if s == 2 and 2 <= c <= C_Z and c % 2 == 0:
                    j = c // 2 - 1
                    copy_pairs(f"y{j}", lambda i: y_pad[:, 4 * j + 2 * i:4 * j + 2 * i + 2, PAD:PAD + SEQ], 1.0)
                if u == 84:
                    guess("ln")
                if u == 85:
                    act.wait_ge(S["moments_full"], 1)
                    nc.scalar.activation(moments.rearrange("p a b -> p (a b)"), PS[:, 6, :], ACT.Copy)\
                        .then_inc(S["moments_ready"], 1)
                if 86 <= u < 90:
                    j = u - 86
                    want(SILU)
                    act.wait_ge(S["normed"], j + 1)
                    for k in range(4 * j, 4 * j + 4):
                        ins = nc.scalar.activation(conv[:, k, :], conv[:, k, :], ACT.Silu,
                                                   scale=gain("a_ln_g", k), bias=gain("a_ln_b", k))
                    ins.then_inc(S["silu_ready"], 1)
                if u in (73, 80, 90, 96):
                    j = (73, 80, 90, 96).index(u)
                    if j == 0:
                        act.wait_ge(S["y_ready"], 4)
                    if j == 1:
                        transposed(act, "y3")
                    if j >= 2:
                        transposed(act, f"z{j - 2}")
                    evacuate(C_Z + j, stage_at(j % 2), ACT.Silu, r_x)
                if u in (89, 91, 93, 97):
                    j = (89, 91, 93, 97).index(u)
                    for i in range(2):
                        act.wait_ge(S["t_multiplied"], MUL_NO[f"z{j}"] * 2 + i + 1)
                        ins = nc.scalar.activation(hi["B"][:, 4 * j + 2 * i:4 * j + 2 * i + 2, :],
                                                   conv[:, 4 * j + 2 * i:4 * j + 2 * i + 2, :], ACT.Copy)
                        ins.then_inc(S["t_hi_ready"], 1)
                if s == 1 and C_OUT < c <= C_K:
                    j = c - C_OUT - 1
                    hi_parts(f"w{j}", "A", 4 * j, "kv_norm_g")
                if u == FIRST[C_K] + 2:
                    act.wait_ge(S["x1_ready"], 4)
                    squares_of_rows("x1")
                    guess("x1")
                if s == 4 and C_K <= c < C_V:
                    j = c - C_K
                    hi_parts(f"b{j}", "B", 4 * j, "b_norm_g")
                for m, c0, dst, scale in (("k", C_K, k_t, 1.0), ("q", C_Q, q_t, qk_gain)):
                    if s == 0 and c0 < c <= c0 + 4:
                        j = c - c0 - 1
                        chunk_done(act, c - 1)
                        if j >= 2:
                            transposed(act, f"{m}{j - 2}")
                        elif m == "k" and j == 0:
                            transposed(act, "z3")
                            act.wait_ge(S["x1_scale_ready"], 1)
                        elif m == "q":
                            transposed(act, f"k{j + 2}")
                        for tok in range(TT):
                            ins = nc.scalar.activation(stage[:, j % 2, tok, :], chunk_bank(c - 1, tok),
                                                       ACT.Square, scale=r_x1[:, tok:tok + 1])
                        ins.then_inc(S["sumsq_ready"], 1)
                        guess(f"{m}{j}")
                    if s == 2 and c0 < c <= c0 + 4:
                        j = c - c0 - 1
                        copy_pairs(f"{m}{j}", lambda i: dst[:, 4 * j + 2 * i:4 * j + 2 * i + 2, :], scale)
                if s == 0 and C_V < c <= C_V + 4:
                    j = c - C_V - 1
                    evacuate(c - 1, lambda tok: vals[:, tok, j * NC:(j + 1) * NC], ACT.Copy, r_x1)
                h, b = divmod(u - DIFF_FROM, DIFF_STEP)
                if 0 <= h < HEADS:
                    if b == 1:
                        want(EXP_LN)
                        act.wait_ge(S["d_negmax"], h + 1)
                        for m in range(2):
                            for tok, (f, e) in enumerate(((0, 128), (128, 384))):
                                i = 2 * m + tok
                                ins = nc.scalar.activation(work[:, m, f:e], PS[:, 6 + m, f:e], ACT.Exp,
                                                           bias=neg_max[:, i:i + 1],
                                                           accum_out=sums[:, i:i + 1])
                        ins.then_inc(S["d_exp"], 1)
                    if b == 3:
                        act.wait_ge(S["d_pt"], h + 1)
                        nc.scalar.activation(probs_t[:, :], PS[:, 6, 0:384], ACT.Copy)\
                            .then_inc(S["d_pt_copied"], 1)
                h, b = divmod(u - DIFF_FROM - DIFF_STEP, DIFF_STEP)
                if 0 <= h < HEADS and b == 0:
                    act.wait_ge(S["on_ready"], h + 1)
                    for tok in range(TT):
                        ins = nc.scalar.activation(work[:, tok, 0:2 * DH], heads_out[:, h % 4, tok, :],
                                                   ACT.Square, accum_out=root[f"o{h}"]["ss"][:, tok:tok + 1])
                    ins.then_inc(S["sumsq_ready"], 1)
                    guess(f"o{h}")
                if s == 0 and C_ZB < c <= C_OUTB:
                    j = c - C_ZB - 1
                    if j < 2:
                        transposed(act, f"q{j + 2}")
                    else:
                        act.wait_ge(S["d_gated"], j - 1)
                    evacuate(c - 1, stage_at(j % 2), ACT.Silu, r_x1)
                    want(EXP_LN)
                if u in OG_AT:
                    j = OG_AT.index(u)
                    transposed(act, f"og{j}")
                    for i in range(4):
                        ins = nc.scalar.activation(act_hi("A", 4 * j + i), bank_pair(i // 2)[:, i % 2, :],
                                                   ACT.Copy, scale=sub_gain[:, i % 2:i % 2 + 1])
                        if i % 2:
                            ins.then_inc(S["t_hi_ready"], 1)
                if s == 1 and C_OUTB < c <= C_CQ:
                    j = c - C_OUTB - 1
                    hi_parts(f"v{j}", "B", 4 * j, "pre_norm_w_2")
                if u == FIRST[C_CQ] + 2:
                    act.wait_ge(S["x2_ready"], 4)
                    squares_of_rows("x2")
                    guess("x2")
                if u == FIRST[C_CKV]:
                    chunk_done(act, C_CQ)
                    act.wait_ge(S["x2_scale_ready"], 1)
                    squares_of_chunk(C_CQ, 512, "cq", r_x2)
                    guess("cq")
                    act.wait_ge(S["cq_scale"], 1)
                    evacuate(C_CQ, stage_at(0), ACT.Copy, cq_scale)
                if u == FIRST[C_CKV] + 2:
                    hi_parts("cq", "A", 0, "q_norm_w_2")
                if u == FIRST[C_QUP]:
                    chunk_done(act, C_CKV)
                    squares_of_chunk(C_CKV, 256, "ckv", r_x2)
                    for tok in range(TT):
                        ins = nc.scalar.activation(stage[:, 1, tok, 256:320],
                                                   PS[:, 2 * (C_CKV % 2) + tok, 256:320], ACT.Copy,
                                                   scale=r_x2[:, tok:tok + 1])
                    ins.then_inc(S["kr_staged"], 1)
                    guess("ckv")
                    act.wait_ge(S["ckv_scale"], 1)
                    evacuate(C_CKV, lambda tok: stage[:, 1, tok, 0:256], ACT.Copy, ckv_scale, w=256)
                if u == FIRST[C_QUP] + 2:
                    transposed(act, "ckv")
                    nc.scalar.activation(kr_t[0:ROT, :], PS[0:ROT, 5, 0:SEQ], ACT.Copy)
                    for i in range(2):
                        ins = nc.scalar.activation(act_hi("A", 4 + i), bank_pair(0)[:, i, :],
                                                   ACT.Copy, scale=gain("kv_norm_w_2", i))
                    ins.then_inc(S["t_hi_ready"], 1)
                if s == 0 and C_QUP < c <= C_KVUP:
                    j = c - C_QUP - 1
                    chunk_done(act, c - 1)
                    if j >= 2:
                        transposed(act, f"qu{j - 2}")
                    for tok in range(TT):
                        ins = nc.scalar.activation(qu_stage[:, j % 2, tok, :], chunk_bank(c - 1, tok), ACT.Copy)
                    ins.then_inc(S["chunk_read_act"], 1)
                for j in range(4):
                    if u == FIRST[C_QUP + j + 1] + 1:
                        transposed(act, f"qu{j}")
                        nc.scalar.activation(qn_t[:, 2 * j:2 * j + 2, :], bank_pair(0), ACT.Copy,
                                             scale=float(192 ** -0.5))
                        nc.scalar.activation(qr_t[0:ROT, 2 * j:2 * j + 2, :], bank_pair(1)[0:ROT], ACT.Copy,
                                             scale=float(192 ** -0.5)).then_inc(S["t_copied"], 1)
                if s == 0 and C_KVUP < c <= C_SBQ:
                    j = c - C_KVUP - 1
                    chunk_done(act, c - 1)
                    if j == 0:
                        transposed(act, "cq")
                    elif j == 1:
                        transposed(act, "ckv")
                    else:
                        transposed(act, f"ku{j - 2}")
                    for tok in range(TT):
                        kv = chunk_bank(c - 1, tok).rearrange("p (h m n) -> p h m n", h=2, m=2)
                        nc.scalar.activation(stage[:, j % 2, tok, 0:256].rearrange("p (h n) -> p h n", h=2),
                                             kv[:, :, 0, :], ACT.Copy)
                        ins = nc.scalar.activation(v_mla[:, tok, 256 * j:256 * j + 256]
                                                   .rearrange("p (h n) -> p h n", h=2),
                                                   kv[:, :, 1, :], ACT.Copy)
                    ins.then_inc(S["chunk_read_act"], 1)
                for j in range(4):
                    if u == FIRST[C_KVUP + j + 1] + 1:
                        copy_pairs(f"ku{j}", lambda i: kn_t[:, 2 * j:2 * j + 2, :], 1.0, n=1)
                for m, c0, dst, scale in (("sq", C_SBQ, sq_t, float(DH ** -0.5)), ("sk", C_SBK, sk_t, 1.0)):
                    if s == 0 and c0 < c <= c0 + 2:
                        j = c - c0 - 1
                        transposed(act, f"ku{j + 2}" if m == "sq" else f"sq{j}")
                        evacuate(c - 1, stage_at(j), ACT.Copy, r_x2)
                    if s == 2 and c0 < c <= c0 + 2:
                        j = c - c0 - 1
                        copy_pairs(f"{m}{j}", lambda i: dst[:, 4 * j + 2 * i:4 * j + 2 * i + 2, :], scale)
                if s == 0 and C_SBV < c <= C_SBV + 2:
                    j = c - C_SBV - 1
                    evacuate(c - 1, lambda tok: v_sb[:, tok, j * NC:(j + 1) * NC], ACT.Copy, r_x2)
                h, b = divmod(u - MLA_FROM, MLA_STEP)
                if 0 <= h < HEADS:
                    if b == 0:
                        act.wait_ge(S["m_negmax"], h + 1)
                        for tok, (f, e) in enumerate(((0, 128), (128, 384))):
                            ins = nc.scalar.activation(work[:, h % 2, f:e], PS[:, 6, f:e], ACT.Exp,
                                                       bias=neg_max[:, tok:tok + 1],
                                                       accum_out=sums[:, tok:tok + 1])
                        ins.then_inc(S["m_exp"], 1)
                    if b == 2:
                        act.wait_ge(S["m_pt"], h + 1)
                        nc.scalar.activation(probs_t[:, :], PS[:, 7, 0:384], ACT.Copy)\
                            .then_inc(S["m_pt_copied"], 1)
                    if b == 3:
                        act.wait_ge(S["m_out"], h + 1)
                        nc.scalar.activation(qn_t[:, h, :], PS[:, 6, 0:SEQ], ACT.Copy)\
                            .then_inc(S["m_out_copied"], 1)
                for m, c0, k0 in (("mg", C_MG, 8), ("sg", C_SG, 0)):
                    if s == 0 and c0 < c <= c0 + 2:
                        j = c - c0 - 1
                        transposed(act, f"sk{j}" if m == "mg" else f"mg{j}")
                        evacuate(c - 1, stage_at(j), ACT.Silu, r_x2)
                        want(EXP_LN)
                    if s == 2 and c0 < c <= c0 + 2:
                        j = c - c0 - 1
                        gated = qn_t if m == "mg" else sq_t
                        for i in range(2):
                            act.wait_ge(S["t_multiplied"], MUL_NO[f"{m}{j}"] * 2 + i + 1)
                            nc.scalar.activation(hi["A"][:, k0 + 4 * j + 2 * i:k0 + 4 * j + 2 * i + 2, :],
                                                 gated[:, 4 * j + 2 * i:4 * j + 2 * i + 2, :], ACT.Copy)\
                                .then_inc(S["t_hi_ready"], 1)
                h, b = divmod(u - SB_FROM, SB_STEP)
                if 0 <= h < HEADS:
                    if b == 0:
                        act.wait_ge(S["s_scores"], h + 1)
                        link(nc.scalar.activation(work[:, 0, :], PS[:, 6, 0:384], ACT.Abs))
                        link(nc.scalar.activation(work[:, 0, :], work[:, 0, :], ACT.Exp, scale=-1.0))
                        nc.scalar.activation(work[:, 0, :], work[:, 0, :], ACT.Ln, bias=1.0)\
                            .then_inc(S["s_soft"], 1)
                    if b == 2:
                        act.wait_ge(S["s_logit"], h + 1)
                        nc.scalar.activation(work[:, 0, :], probs_t[:, :], ACT.Exp).then_inc(S["s_weight"], 1)
                    if b == 3:
                        act.wait_ge(S["s_out"], h + 1)
                        nc.scalar.activation(sq_t[:, h, :], PS[:, 6, 0:SEQ], ACT.Copy)\
                            .then_inc(S["s_out_copied"], 1)
                if s == 0 and c > C_OUT2:
                    j = c - C_OUT2 - 1
                    chunk_done(act, c - 1)
                    for tok in range(TT):
                        ins = nc.scalar.activation(work[:, :, :].rearrange("p a b -> p (a b)")[:, 0:NC],
                                                   chunk_bank(c - 1, tok), ACT.Square,
                                                   accum_out=y_sums[:, 4 * tok + j:4 * tok + j + 1])
                        if tok == 0:
                            link(ins)
                    ins.then_inc(S["y_squared"], 1)
                split(u + AHEAD)
            chunk_done(act, NCH - 1)
            for tok in range(TT):
                ins = nc.scalar.activation(work[:, :, :].rearrange("p a b -> p (a b)")[:, 0:NC],
                                           chunk_bank(NCH - 1, tok), ACT.Square,
                                           accum_out=y_sums[:, 4 * tok + 3:4 * tok + 4])
                if tok == 0:
                    link(ins)
            ins.then_inc(S["y_squared"], 1)
            guess("post")

        @block.vector
        def _(dve):
            n_chain = [0]
            V = nc.vector

            def note(ins):
                n_chain[0] += 1
                ins.then_inc(S["dve_chain"], 1)
                return n_chain[0]

            def link(ins):
                dve.wait_ge(S["dve_chain"], note(ins))

            def split(u):
                if u >= NU or WHOLE[u]:
                    return
                n, w = SPLIT_NO[u], CHUNKS[UNITS[u][0]][2]
                dve.wait_ge(S["w_hi_ready"], n + 1)
                V.tensor_tensor(w_lo[:, n % PARTS, 0:2 * w], w_raw[:, u % RAW, 0:2 * w],
                                w_hi[:, n % PARTS, 0:2 * w].bitcast(F32), ALU.subtract)\
                    .then_inc(S["w_lo_ready"], 1)

            n_hi = [0]

            def hi_bank():
                n_hi[0] += 1
                dve.wait_ge(S["t_hi_ready"], n_hi[0])

            def lo_parts(which, k0, g, n=4, whole=False):
                for i in range(n):
                    if i % 2 == 0:
                        hi_bank()
                    ins = V.scalar_tensor_tensor(lo[which][:, k0 + i, :], bank_pair(i // 2)[:, i % 2, :], g(i),
                                                 hi[which][:, k0 + i, :].bitcast(F32), ALU.mult, ALU.subtract)
                    if whole:
                        ins = V.tensor_scalar(x_t[:, k0 + i, :], bank_pair(i // 2)[:, i % 2, :], g(i), None,
                                              ALU.mult)
                ins.then_inc(S["lo_ready"], 1)

            def gated_parts(name, src, k_src, which, k0, gate_ready):
                transposed(dve, name)
                gate_ready()
                for i in range(2):
                    a = src[:, k_src + 2 * i:k_src + 2 * i + 2, :]
                    V.tensor_tensor(a, bank_pair(i), a, ALU.mult).then_inc(S["t_multiplied"], 1)
                for i in range(2):
                    hi_bank()
                    ins = V.tensor_tensor(lo[which][:, k0 + 2 * i:k0 + 2 * i + 2, :],
                                          src[:, k_src + 2 * i:k_src + 2 * i + 2, :],
                                          hi[which][:, k0 + 2 * i:k0 + 2 * i + 2, :].bitcast(F32), ALU.subtract)
                ins.then_inc(S["lo_ready"], 1)

            def variance(name, scale, wait=True):
                if wait:
                    dve.wait_ge(S["sumsq_ready"], SS_NO[name] + 1)
                V.tensor_scalar(root[name]["v"], root[name]["ss"], scale, EPS, ALU.mult, ALU.add)\
                    .then_inc(S["var_ready"], 1)

            def refine(name):
                r = root[name]
                dve.wait_ge(S["guess_ready"], RS_NO[name] + 1)
                link(V.tensor_tensor(r["t"], r["y"], r["y"], ALU.mult))
                link(V.tensor_tensor(r["t"], r["t"], r["v"], ALU.mult))
                link(V.tensor_scalar(r["t"], r["t"], -0.5, 1.5, ALU.mult, ALU.add))
                return V.tensor_tensor(r["r"], r["y"], r["t"], ALU.mult)

            def add_residual(c, name):
                chunk_done(dve, c)
                j = (c - C_OUT) % 4
                for tok in range(TT):
                    a = x_res[:, tok, j * NC:(j + 1) * NC]
                    ins = V.tensor_tensor(a, chunk_bank(c, tok), a, ALU.add)
                ins.then_inc(S[name], 1)

            dve.wait_ge(S["consts_ready"], 2)
            dve.wait_ge(S["rows_loaded"], 16 * 15)
            lam_rows = work[:, :, :].rearrange("p a b -> p (a b)")[:, 0:4 * DH]\
                .rearrange("p (i j d) -> p i j d", i=2, j=2)
            lam_prod = probs_t[:, 0:2 * DH].rearrange("p (i d) -> p i d", i=2)
            link(V.tensor_tensor(lam_prod, lam_rows[:, :, 0, :], lam_rows[:, :, 1, :], ALU.mult))
            V.tensor_reduce(lam_sums, lam_prod, AX.X, ALU.add).then_inc(S["lam_in"], 1)
            link(V.tensor_copy(pos_f, pos_i[:, :]))
            for tok in range(TT):
                n = note(V.tensor_scalar(rope[:, 1, tok, :], rope[:, 7, 0, :], pos_f[:, tok:tok + 1], None,
                                         ALU.mult))
            dve.wait_ge(S["dve_chain"], n)
            link(V.tensor_scalar(rope[:, 0, :, :], rope[:, 1, :, :], 1 / (2 * math.pi), ROUND,
                                 ALU.mult, ALU.add))
            link(V.tensor_scalar(rope[:, 0, :, :], rope[:, 0, :, :], ROUND, None, ALU.subtract))
            for part in (PI_A, PI_B, PI_C):
                link(V.scalar_tensor_tensor(rope[:, 1, :, :], rope[:, 0, :, :], -part, rope[:, 1, :, :],
                                            ALU.mult, ALU.add))
            V.tensor_scalar(rope[:, 0, :, :], rope[:, 1, :, :], PI_LOW, -PI_LOW, ALU.min, ALU.max)\
                .then_inc(S["angle_ready"], 1)
            dve.wait_ge(S["tables_ready"], 1)
            link(V.tensor_tensor(qk_gain, gain("k_norm_g", 0), gain("b_q_norm_g", 0), ALU.mult))
            link(V.tensor_scalar(qk_gain, qk_gain, float(DH ** -0.5), None, ALU.mult))
            r_sub = ROWS["b_subln_g"][0]
            note(V.tensor_scalar(sub_gain, gains[:, r_sub:r_sub + 2], 1.0 - LAM_INIT, None, ALU.mult))

            def gain_of(name, k0):
                return lambda i: gain(name, k0 + i)

            for j in range(4):
                lo_parts("A", 4 * j, gain_of("a_norm_g", 4 * j), whole=True)
                if j < AHEAD:
                    split(j)
            variance("x", 1.0 / D)
            refine("x").then_inc(S["x_scale_ready"], 1)
            dve.wait_ge(S["lam_exp"], 1)
            link(V.tensor_tensor(neg_lam, lam_exps[:, 1:2], lam_exps[:, 0:1], ALU.subtract))
            note(V.tensor_scalar(neg_lam, neg_lam, -LAM_INIT, None, ALU.add))
            dve.wait_ge(S["sines_ready"], 1)
            link(V.tensor_tensor(rope[:, 3, :, :], rope[:, 3, :, :], rope[:, 3, :, :], ALU.mult))
            link(V.tensor_scalar(rope[:, 3, :, :], rope[:, 3, :, :], -2.0, 1.0, ALU.mult, ALU.add))
            sin_t, cos_t = rope[:, 2, :, :], rope[:, 3, :, :]

            r_x1, r_x2 = root["x1"]["r"], root["x2"]["r"]
            tap_list = [(k + i, tap) for k in range(0, KT, 2) for tap in range(TAPS) for i in range(2)]
            tap_at = [0]
            tap_done = {}
            refined = {}

            def convolve(j, n):
                end = min(tap_at[0] + n, (j + 1) * 4 * TAPS)
                for k, tap in tap_list[tap_at[0]:end]:
                    src = y_pad[:, k, tap:tap + SEQ]
                    if tap == 0:
                        ins = V.tensor_scalar(conv[:, k, :], src, taps[:, k, 0:1], gain("a_dw_b", k),
                                              ALU.mult, ALU.add)
                    else:
                        dve.wait_ge(S["dve_chain"], tap_done[k])
                        ins = V.scalar_tensor_tensor(conv[:, k, :], src, taps[:, k, tap:tap + 1],
                                                     conv[:, k, :], ALU.mult, ALU.add)
                    if tap == TAPS - 1 and k % 4 == 3:
                        ins.then_inc(S["conv_ready"], 1)
                    else:
                        tap_done[k] = note(ins)
                tap_at[0] = end

            def scale_heads(c, j, m):
                name = f"{m}{j}"
                dve.wait_ge(S["sumsq_ready"], SS_NO[name] + 1)
                for tok in range(TT):
                    n = note(V.tensor_reduce(root[name]["ss"][:, 4 * tok:4 * tok + 4],
                                             stage[:, j % 2, tok, :].rearrange("p (h d) -> p h d", h=4),
                                             AX.X, ALU.add))
                dve.wait_ge(S["dve_chain"], n)
                variance(name, 1.0 / DH, wait=False)
                link(refine(name))
                for tok in range(TT):
                    n = note(V.tensor_scalar(k_scale[name][:, 4 * tok:4 * tok + 4],
                                             root[name]["r"][:, 4 * tok:4 * tok + 4],
                                             r_x1[:, tok:tok + 1], None, ALU.mult))
                dve.wait_ge(S["dve_chain"], n)
                for tok in range(TT):
                    sc = k_scale[name][:, 4 * tok:4 * tok + 4].unsqueeze(2).to_broadcast([P, 4, DH])
                    ins = V.tensor_tensor(stage[:, j % 2, tok, :].rearrange("p (h d) -> p h d", h=4),
                                          chunk_bank(c, tok).rearrange("p (h d) -> p h d", h=4), sc, ALU.mult)
                ins.then_inc(S["chunk_read_dve"], 1)

            def rotate(a, heads, tmp):
                x1, x2 = a[:, :, :, 0:32], a[:, :, :, 32:64]
                shape = [P, TT, heads, 32]
                co = cos_t.unsqueeze(2).to_broadcast(shape)
                si = sin_t.unsqueeze(2).to_broadcast(shape)
                t1, t2 = tmp
                note(V.tensor_tensor(t1, x1, si, ALU.mult))
                link(V.tensor_tensor(t2, x2, si, ALU.mult))
                note(V.tensor_tensor(x1, x1, co, ALU.mult))
                link(V.tensor_tensor(x2, x2, co, ALU.mult))
                note(V.tensor_tensor(x1, x1, t2, ALU.subtract))
                return V.tensor_tensor(x2, x2, t1, ALU.add)

            for u, (c, s) in enumerate(UNITS):
                if s == 0 and 2 <= c <= C_Z and c % 2 == 0:
                    j = c // 2 - 1
                    dve.wait_ge(S["sig_ready"], j + 1)
                    V.tensor_tensor(stage[:, 1, :, :], stage[:, 0, :, :], stage[:, 1, :, :], ALU.mult)\
                        .then_inc(S["y_ready"], 1)
                for j, f in enumerate(CONV_FROM):
                    if f <= u < f + CONV_SLOTS:
                        if u == f:
                            dve.wait_ge(S["t_copied"], COPY_NO[f"y{j}"] + 1)
                        convolve(j, CONV_RATE)
                    if u == f + CONV_SLOTS + 1:
                        for tok in range(TT):
                            dve.wait_ge(S["stats_full"], 2 * j + tok + 1)
                            g = 4 * tok + j
                            ins = V.bn_stats(bn[:, 6 * g:6 * g + 6], PS[:, 6 + tok, :])
                            ins.then_inc(S["stats_read"], 1)
                if u == 84:
                    dve.wait_ge(S["stats_read"], 8)
                    for tok in range(TT):
                        n = note(V.bn_aggr(mv[:, 2 * tok:2 * tok + 2], bn[:, 24 * tok:24 * tok + 24]))
                    dve.wait_ge(S["dve_chain"], n)
                    V.tensor_scalar(root["ln"]["v"], mv[:, 1:4:2], 1.0, EPS, ALU.mult, ALU.add)\
                        .then_inc(S["var_ready"], 1)
                    link(refine("ln"))
                    for tok in range(TT):
                        V.tensor_scalar(diag[:, tok, :], ident[:, :], mv[:, 2 * tok:2 * tok + 1], None, ALU.mult)
                        ins = V.tensor_scalar(diag[:, 2 + tok, :], ident[:, :],
                                              root["ln"]["r"][:, tok:tok + 1], None, ALU.mult)
                    ins.then_inc(S["diag_ready"], 1)
                if u == 85:
                    dve.wait_ge(S["moments_ready"], 1)
                    mean = moments[:, 0:1, :].to_broadcast([P, 4, SEQ])
                    inv = moments[:, 1:2, :].to_broadcast([P, 4, SEQ])
                    for j in range(4):
                        a = conv[:, 4 * j:4 * j + 4, :]
                        link(V.tensor_tensor(a, a, mean, ALU.subtract))
                        V.tensor_tensor(a, a, inv, ALU.mult).then_inc(S["normed"], 1)
                if u in (89, 91, 93, 97):
                    j = (89, 91, 93, 97).index(u)
                    gated_parts(f"z{j}", conv, 4 * j, "B", 4 * j,
                                lambda: dve.wait_ge(S["silu_ready"], j + 1))
                if s == 0 and C_OUT < c <= C_K:
                    add_residual(c - 1, "x1_ready")
                if s == 1 and C_OUT < c <= C_K:
                    lo_parts("A", 4 * (c - C_OUT - 1), gain_of("kv_norm_g", 4 * (c - C_OUT - 1)))
                if u == FIRST[C_K] + 2:
                    variance("x1", 1.0 / D)
                    refine("x1").then_inc(S["x1_scale_ready"], 1)
                if s == 4 and C_K <= c < C_V:
                    lo_parts("B", 4 * (c - C_K), gain_of("b_norm_g", 4 * (c - C_K)))
                if s == 0 and C_K < c <= C_V:
                    if c == C_K + 1:
                        dve.wait_ge(S["x1_scale_ready"], 1)
                    scale_heads(c - 1, c - C_K - 1, "k")
                if s == 0 and C_Q < c <= C_ZB:
                    scale_heads(c - 1, c - C_Q - 1, "q")
                h, b = divmod(u - DIFF_FROM, DIFF_STEP)
                if 0 <= h < HEADS:
                    if b == 0:
                        dve.wait_ge(S["d_scores"], h + 1)
                        V.reduce_max(neg_max[:, 0:4:2], PS[:, 6:8, 0:128], AX.X, negate=True)
                        V.reduce_max(neg_max[:, 1:4:2], PS[:, 6:8, 128:384], AX.X, negate=True)\
                            .then_inc(S["d_negmax"], 1)
                    if b == 2:
                        dve.wait_ge(S["d_exp"], h + 1)
                        link(V.reciprocal(recips, sums))
                        link(V.tensor_scalar(neg_r, recips[:, 2:4], neg_lam, None, ALU.mult))
                        for tok, (f, e) in enumerate(((0, 128), (128, 384))):
                            n = note(V.tensor_scalar(work[:, 1, f:e], work[:, 1, f:e], neg_r[:, tok:tok + 1],
                                                     None, ALU.mult))
                        dve.wait_ge(S["dve_chain"], n)
                        for tok, (f, e) in enumerate(((0, 128), (128, 384))):
                            ins = V.scalar_tensor_tensor(work[:, 0, f:e], work[:, 0, f:e],
                                                         recips[:, tok:tok + 1], work[:, 1, f:e],
                                                         ALU.mult, ALU.add)
                        ins.then_inc(S["d_probs"], 1)
                    if b == 4:
                        dve.wait_ge(S["d_out"], h + 1)
                        V.tensor_copy(heads_out[:, h % 4, :, :],
                                      PS[:, 7, :].rearrange("p (t n) -> p t n", t=TT))\
                            .then_inc(S["on_ready"], 1)
                h, b = divmod(u - DIFF_FROM - DIFF_STEP, DIFF_STEP)
                if 0 <= h < HEADS and b == 0:
                    variance(f"o{h}", 1.0 / (2 * DH))
                if 0 <= h < HEADS and b == 1:
                    refined[h] = note(refine(f"o{h}"))
                if u in GATE_AT:
                    j = GATE_AT.index(u)
                    dve.wait_ge(S["chunk_read_act"], acts_up_to(C_ZB + j))
                    dve.wait_ge(S["dve_chain"], refined[2 * j + 1])
                    for h in (2 * j, 2 * j + 1):
                        for tok in range(TT):
                            a = heads_out[:, h % 4, tok, :]
                            ins = V.scalar_tensor_tensor(
                                a, a, root[f"o{h}"]["r"][:, tok:tok + 1],
                                stage[:, j % 2, tok, 256 * (h % 2):256 * (h % 2) + 256], ALU.mult, ALU.mult)
                    ins.then_inc(S["d_gated"], 1)
                if u in OG_AT:
                    lo_parts("A", 4 * OG_AT.index(u), lambda i: sub_gain[:, i % 2:i % 2 + 1])
                if s == 0 and C_OUTB < c <= C_CQ:
                    add_residual(c - 1, "x2_ready")
                if s == 1 and C_OUTB < c <= C_CQ:
                    lo_parts("B", 4 * (c - C_OUTB - 1), gain_of("pre_norm_w_2", 4 * (c - C_OUTB - 1)))
                if u == FIRST[C_CQ] + 2:
                    variance("x2", 1.0 / D)
                    refine("x2").then_inc(S["x2_scale_ready"], 1)
                if u == FIRST[C_CKV]:
                    variance("cq", 1.0 / 512)
                    link(refine("cq"))
                    V.tensor_tensor(cq_scale, root["cq"]["r"], r_x2, ALU.mult).then_inc(S["cq_scale"], 1)
                if u == FIRST[C_CKV] + 2:
                    lo_parts("A", 0, gain_of("q_norm_w_2", 0))
                if u == FIRST[C_QUP]:
                    variance("ckv", 1.0 / 256)
                    link(refine("ckv"))
                    V.tensor_tensor(ckv_scale, root["ckv"]["r"], r_x2, ALU.mult).then_inc(S["ckv_scale"], 1)
                    dve.wait_ge(S["kr_staged"], 1)
                    rotate(stage[:, 1, :, 256:320].unsqueeze(2), 1,
                           (rope[:, 4, :, :].unsqueeze(2), rope[:, 5, :, :].unsqueeze(2)))\
                        .then_inc(S["kr_roped"], 1)
                if u == FIRST[C_QUP] + 2:
                    lo_parts("A", 4, gain_of("kv_norm_w_2", 0), n=2)
                if s == 0 and C_QUP < c <= C_KVUP:
                    j = c - C_QUP - 1
                    dve.wait_ge(S["chunk_read_act"], acts_up_to(c - 1))
                    tmp = [rope[:, i, :, :] for i in (4, 5, 0, 1)]
                    for h in range(2):
                        a = qu_stage[:, j % 2, :, h * 192 + DH:h * 192 + DH + ROT].unsqueeze(2)
                        ins = rotate(a, 1, (tmp[2 * h].unsqueeze(2), tmp[2 * h + 1].unsqueeze(2)))
                        if h == 0:
                            note(ins)
                    ins.then_inc(S["qu_roped"], 1)
                h, b = divmod(u - MLA_FROM, MLA_STEP)
                if 0 <= h < HEADS:
                    if b == 0:
                        dve.wait_ge(S["m_scores"], h + 1)
                        V.reduce_max(neg_max[:, 0:1], PS[:, 6, 0:128], AX.X, negate=True)
                        V.reduce_max(neg_max[:, 1:2], PS[:, 6, 128:384], AX.X, negate=True)\
                            .then_inc(S["m_negmax"], 1)
                    if b == 1:
                        m = h % 2
                        dve.wait_ge(S["m_exp"], h + 1)
                        link(V.reciprocal(recips[:, 0:2], sums[:, 0:2]))
                        for tok, (f, e) in enumerate(((0, 128), (128, 384))):
                            ins = V.tensor_scalar(work[:, m, f:e], work[:, m, f:e], recips[:, tok:tok + 1],
                                                  None, ALU.mult)
                        ins.then_inc(S["m_probs"], 1)
                for m, c0, k0 in (("mg", C_MG, 8), ("sg", C_SG, 0)):
                    if s == 2 and c0 < c <= c0 + 2:
                        j = c - c0 - 1
                        src, done = (qn_t, "m_out_copied") if m == "mg" else (sq_t, "s_out_copied")
                        gated_parts(f"{m}{j}", src, 4 * j, "A", k0 + 4 * j,
                                    lambda: dve.wait_ge(S[done], 4 * j + 4))
                h, b = divmod(u - SB_FROM, SB_STEP)
                if 0 <= h < HEADS:
                    z = PS[:, 6, 0:384]

                    def mask_strict(a):
                        a = a.rearrange("p (b n) -> p b n", n=P)[:, 0:3:2, :]
                        return V.tensor_tensor(a, a, strict[:, :].unsqueeze(1).to_broadcast([P, 2, P]), ALU.mult)
                    if b == 1:
                        dve.wait_ge(S["s_soft"], h + 1)
                        link(V.scalar_tensor_tensor(work[:, 1, :], z, 0.0, work[:, 0, :], ALU.max, ALU.add))
                        link(V.tensor_tensor(probs_t[:, :], z, work[:, 1, :], ALU.subtract))
                        mask_strict(work[:, 1, :]).then_inc(S["s_keep"], 1)
                    if b == 2:
                        dve.wait_ge(S["s_later"], h + 1)
                        V.tensor_tensor(probs_t[:, :], PS[:, 7, 0:384], probs_t[:, :], ALU.add)\
                            .then_inc(S["s_logit"], 1)
                        dve.wait_ge(S["s_weight"], h + 1)
                        mask_strict(work[:, 0, :]).then_inc(S["s_masked"], 1)
                if s == 0 and c > C_OUT2:
                    scale_output(nc, S, dve, c - 1, c - C_OUT2 - 1, chunk_bank, yw, post_gain)
                split(u + AHEAD)
            scale_output(nc, S, dve, NCH - 1, 3, chunk_bank, yw, post_gain)
            link(V.tensor_reduce(root["post"]["ss"], y_sums.rearrange("p (t j) -> p t j", t=TT), AX.X, ALU.add))
            variance("post", 1.0 / D, wait=False)
            link(refine("post"))
            for j in range(4):
                for tok in range(TT):
                    a = yw[:, tok, j * NC:(j + 1) * NC]
                    V.scalar_tensor_tensor(a, a, root["post"]["r"][:, tok:tok + 1],
                                           x_res[:, tok, j * NC:(j + 1) * NC], ALU.mult, ALU.add)\
                        .then_inc(S["final_ready"], 1)

        @block.tensor
        def _(pe):
            T = nc.tensor

            def t_free(name):
                n = T_NO[name]
                if n == 0:
                    return
                prev, kind = T_EVENTS[n - 1]
                if kind == "copy":
                    pe.wait_ge(S["t_copied"], COPY_NO[prev] + 1)
                elif kind == "mul":
                    pe.wait_ge(S["t_multiplied"], 2 * MUL_NO[prev] + 2)
                else:
                    pe.wait_ge(S["lo_ready"], LO_NO[prev] + 1)

            def transpose_chunk(name, src, n=4):
                t_free(name)
                for i in range(n):
                    for tok in range(TT):
                        at = (i % 2) * SEQ + tok * P
                        ins = T.transpose(PS[:, 4 + i // 2, at:at + P], src(tok, i), ident[:, :])
                ins.then_inc(S["t_full"], 1)

            pieces = [(0, 64, 0, 0, False), (64, P, 0, 64, True),
                      (P, 320, P, 0, False), (320, 384, P, 192, True)]

            def masked_scores(bank, operands):
                for f, e, q0, k0, masked in pieces:
                    for i, (q, k) in enumerate(operands):
                        ins = T.matmul(PS[:, bank, f:e], q[:, q0:q0 + P], k[:, k0:k0 + e - f],
                                       start=i == 0, stop=not masked and i == len(operands) - 1)
                    if masked:
                        ins = T.matmul(PS[:, bank, f:e], mask_row[0:1, 0:P], mask_row[0:1, P:P + 64],
                                       start=False, stop=True)
                return ins

            def staged(buf):
                return lambda tok, i: stage[:, buf, tok, i * P:(i + 1) * P]

            def rows(j):
                return lambda tok, i: x_res[:, tok, j * NC + i * P:j * NC + (i + 1) * P]

            source = {}
            for c in range(NCH):
                for k in range(KT):
                    g = k // 4
                    if c < C_OUT:
                        source[c, k] = f"x{g}"
                    elif c < C_K:
                        source[c, k] = f"z{g}"
                    elif c < C_Q:
                        source[c, k] = f"w{g}"
                    elif c < C_OUTB:
                        source[c, k] = f"b{g}"
                    elif c < C_CQ:
                        source[c, k] = f"og{g}"
                    elif C_QUP <= c < C_KVUP:
                        source[c, k] = "cq"
                    elif C_KVUP <= c < C_SBQ:
                        source[c, k] = "ckv"
                    elif c >= C_OUT2:
                        source[c, k] = f"sg{g}" if g < 2 else f"mg{g - 2}"
                    else:
                        source[c, k] = f"v{g}"

            def products(u):
                c, i = UNITS[u]
                _, _, w, kts, which, k_first = CHUNKS[c]
                if i == 0 and c >= 2:
                    if c - 2 in BY_DVE:
                        name, n = dve_reads(c - 2)
                        pe.wait_ge(S[name], n)
                    else:
                        pe.wait_ge(S["chunk_read_act" if c - 2 not in B_CHUNKS else "y_ready"],
                                   acts_up_to(c - 2) if c - 2 not in B_CHUNKS else (c - 1) // 2)
                pe.wait_ge(S["lo_ready"], LO_NO[source[c, kts[2 * i + 1]]] + 1)
                first, last = i == 0, i == len(kts) // 2 - 1
                if WHOLE[u]:
                    pe.wait_ge(S[f"w{u % RAW}_loaded"], 16 * (u // RAW + 1))
                    raw = w_view(w_raw, u % RAW, w)
                    for kk in range(2):
                        k = k_first + kts[2 * i + kk]
                        for tok in range(TT):
                            ins = T.matmul(chunk_bank(c, tok), x_t[:, k, tok * P:(tok + 1) * P],
                                           raw[:, kk, :], start=first and kk == 0, stop=last and kk == 1)
                else:
                    n = SPLIT_NO[u]
                    pe.wait_ge(S["w_lo_ready"], n + 1)
                    wh, wl = w_view(w_hi, n % PARTS, w), w_view(w_lo, n % PARTS, w)
                    for kk in range(2):
                        k = k_first + kts[2 * i + kk]
                        for tok in range(TT):
                            ah = hi[which][:, k, tok * P:(tok + 1) * P]
                            al = lo[which][:, k, tok * P:(tok + 1) * P]
                            bank = chunk_bank(c, tok)
                            T.matmul(bank, ah, wh[:, kk, :], start=first and kk == 0, stop=False)
                            T.matmul(bank, ah, wl[:, kk, :], start=False, stop=False)
                            ins = T.matmul(bank, al, wh[:, kk, :], start=False, stop=last and kk == 1)
                ins.then_inc(S["units_done"], 1)

            pe.wait_ge(S["consts_ready"], 2)
            pe.wait_ge(S["rows_loaded"], 16 * 15)
            T.transpose(PS[:, 6, 0:NROWS], stage[0:NROWS, 0, 0, 0:P], ident[0:NROWS, 0:NROWS])
            for k in range(KT):
                ins = T.transpose(PS[:, 7, k * TAPS:(k + 1) * TAPS], junk[0:TAPS, k * P:(k + 1) * P],
                                  ident[0:TAPS, 0:TAPS])
            ins.then_inc(S["tables_full"], 1)
            for j in range(2):
                pe.wait_ge(S[f"x{j}_loaded"], 16)
                transpose_chunk(f"x{j}", rows(j))

            for u, (c, s) in enumerate(UNITS):
                if u in (1, 2):
                    pe.wait_ge(S[f"x{u + 1}_loaded"], 16)
                    transpose_chunk(f"x{u + 1}", rows(u + 1))
                if s == 2 and 2 <= c <= C_Z and c % 2 == 0:
                    j = c // 2 - 1
                    pe.wait_ge(S["y_ready"], j + 1)
                    transpose_chunk(f"y{j}", staged(1))
                for j, f in enumerate(CONV_FROM):
                    if u == f + CONV_SLOTS + 1:
                        pe.wait_ge(S["conv_ready"], j + 1)
                        if j:
                            pe.wait_ge(S["stats_read"], 2 * j)
                        else:
                            pe.wait_ge(S["tables_ready"], 1)
                        for tok in range(TT):
                            for i in range(4):
                                ins = T.transpose(PS[:, 6 + tok, i * P:(i + 1) * P],
                                                  conv[:, 4 * j + i, tok * P:(tok + 1) * P], ident[:, :])
                            ins.then_inc(S["stats_full"], 1)
                if u == 85:
                    pe.wait_ge(S["diag_ready"], 1)
                    for i in range(4):
                        ins = T.matmul(PS[:, 6, i * P:(i + 1) * P], ones[:, :], diag[:, i, :],
                                       start=True, stop=True)
                    ins.then_inc(S["moments_full"], 1)
                if u in (89, 91, 93, 97):
                    j = (89, 91, 93, 97).index(u)
                    pe.wait_ge(S["chunk_read_act"], acts_up_to(C_Z + j))
                    transpose_chunk(f"z{j}", staged(j % 2))
                if s == 1 and C_OUT < c <= C_K:
                    j = c - C_OUT - 1
                    pe.wait_ge(S["x1_ready"], j + 1)
                    transpose_chunk(f"w{j}", rows(j))
                for m, c0 in (("k", C_K), ("q", C_Q)):
                    if s == 2 and c0 < c <= c0 + 4:
                        j = c - c0 - 1
                        pe.wait_ge(S["chunk_read_dve"], j + 1 + (4 if m == "q" else 0))
                        transpose_chunk(f"{m}{j}", staged(j % 2))
                if s == 4 and C_K <= c < C_V:
                    transpose_chunk(f"b{c - C_K}", rows(c - C_K))
                h, b = divmod(u - DIFF_FROM, DIFF_STEP)
                if 0 <= h < HEADS:
                    if b == 0:
                        pe.wait_ge(S["t_copied"], COPY_NO[f"q{h // 2}"] + 1)
                        if h:
                            pe.wait_ge(S["on_ready"], h)
                        for m in range(2):
                            ins = masked_scores(6 + m, [(q_t[:, 2 * h + m, :], k_t[:, 2 * h + m, :])])
                        ins.then_inc(S["d_scores"], 1)
                    if b == 3:
                        pe.wait_ge(S["d_probs"], h + 1)
                        for i in range(3):
                            ins = T.transpose(PS[:, 6, i * P:(i + 1) * P], work[:, 0, i * P:(i + 1) * P],
                                              ident[:, :])
                        ins.then_inc(S["d_pt"], 1)
                    if b == 4:
                        pe.wait_ge(S["d_pt_copied"], h + 1)
                        v0, v1 = (vals[:, i, 256 * h:256 * h + 256] for i in range(2))
                        T.matmul(PS[:, 7, 0:256], probs_t[:, 0:P], v0, start=True, stop=True)
                        T.matmul(PS[:, 7, 256:512], probs_t[:, P:2 * P], v0, start=True, stop=False)
                        T.matmul(PS[:, 7, 256:512], probs_t[:, 2 * P:3 * P], v1, start=False, stop=True)\
                            .then_inc(S["d_out"], 1)
                if u in OG_AT:
                    j = OG_AT.index(u)
                    pe.wait_ge(S["d_gated"], j + 1)
                    transpose_chunk(f"og{j}", lambda tok, i: heads_out[:, (2 * j + i // 2) % 4, tok,
                                                                       (i % 2) * P:(i % 2 + 1) * P])
                if s == 1 and C_OUTB < c <= C_CQ:
                    j = c - C_OUTB - 1
                    pe.wait_ge(S["x2_ready"], j + 1)
                    transpose_chunk(f"v{j}", rows(j))
                if u == FIRST[C_CKV] + 2:
                    pe.wait_ge(S["chunk_read_act"], acts_up_to(C_CQ))
                    transpose_chunk("cq", staged(0))
                if u == FIRST[C_QUP] + 2:
                    pe.wait_ge(S["chunk_read_act"], acts_up_to(C_CKV))
                    pe.wait_ge(S["kr_roped"], 1)
                    t_free("ckv")
                    for tok in range(TT):
                        T.transpose(PS[0:ROT, 5, tok * P:(tok + 1) * P], stage[:, 1, tok, 256:320], ident[:, :])
                    for i in range(2):
                        for tok in range(TT):
                            at = i * SEQ + tok * P
                            ins = T.transpose(PS[:, 4, at:at + P], stage[:, 1, tok, i * P:(i + 1) * P],
                                              ident[:, :])
                    ins.then_inc(S["t_full"], 1)
                for j in range(4):
                    if u == FIRST[C_QUP + j + 1] + 1:
                        pe.wait_ge(S["qu_roped"], j + 1)
                        t_free(f"qu{j}")
                        for h in range(2):
                            for tok in range(TT):
                                at = h * SEQ + tok * P
                                T.transpose(PS[:, 4, at:at + P],
                                            qu_stage[:, j % 2, tok, h * 192:h * 192 + P], ident[:, :])
                                ins = T.transpose(PS[0:ROT, 5, at:at + P],
                                                  qu_stage[:, j % 2, tok, h * 192 + P:h * 192 + 192],
                                                  ident[:, :])
                        ins.then_inc(S["t_full"], 1)
                    if u == FIRST[C_KVUP + j + 1] + 1:
                        pe.wait_ge(S["chunk_read_act"], acts_up_to(C_KVUP + j))
                        transpose_chunk(f"ku{j}", staged(j % 2), n=2)
                for m, c0 in (("sq", C_SBQ), ("sk", C_SBK), ("mg", C_MG), ("sg", C_SG)):
                    if s == 2 and c0 < c <= c0 + 2:
                        j = c - c0 - 1
                        pe.wait_ge(S["chunk_read_act"], acts_up_to(c - 1))
                        transpose_chunk(f"{m}{j}", staged(j))
                h, b = divmod(u - MLA_FROM, MLA_STEP)
                if 0 <= h < HEADS:
                    if b == 0:
                        if h:
                            pe.wait_ge(S["m_out_copied"], h)
                        else:
                            pe.wait_ge(S["t_copied"], COPY_NO["ku3"] + 1)
                        ins = masked_scores(6, [(qn_t[:, h, :], kn_t[:, h, :]),
                                                (qr_t[0:ROT, h, :], kr_t[0:ROT, :])])
                        ins.then_inc(S["m_scores"], 1)
                    if b == 2:
                        pe.wait_ge(S["m_probs"], h + 1)
                        for i in range(3):
                            ins = T.transpose(PS[:, 7, i * P:(i + 1) * P], work[:, h % 2, i * P:(i + 1) * P],
                                              ident[:, :])
                        ins.then_inc(S["m_pt"], 1)
                    if b == 3:
                        pe.wait_ge(S["m_pt_copied"], h + 1)
                        T.matmul(PS[:, 6, 0:SEQ], v_mla[:, 0, h * DH:(h + 1) * DH], probs_t[:, 0:SEQ],
                                 start=True, stop=False)
                        T.matmul(PS[:, 6, P:SEQ], v_mla[:, 1, h * DH:(h + 1) * DH], probs_t[:, SEQ:384],
                                 start=False, stop=True).then_inc(S["m_out"], 1)
                h, b = divmod(u - SB_FROM, SB_STEP)
                if 0 <= h < HEADS:
                    if b == 0:
                        if h:
                            pe.wait_ge(S["s_out_copied"], h)
                        else:
                            pe.wait_ge(S["m_out_copied"], HEADS)
                        T.matmul(PS[:, 6, 0:SEQ], sk_t[:, h, 0:P], sq_t[:, h, :], start=True, stop=True)
                        T.matmul(PS[:, 6, SEQ:384], sk_t[:, h, P:SEQ], sq_t[:, h, P:SEQ], start=True, stop=True)\
                            .then_inc(S["s_scores"], 1)
                    if b == 2:
                        pe.wait_ge(S["s_keep"], h + 1)
                        T.matmul(PS[:, 7, 0:SEQ], after[:, :], work[:, 1, 0:SEQ], start=True, stop=False)
                        T.matmul(PS[:, 7, P:SEQ], neg_ones[:, :], work[:, 1, SEQ:384], start=False, stop=True)
                        T.matmul(PS[:, 7, SEQ:384], after[:, :], work[:, 1, SEQ:384], start=True, stop=True)\
                            .then_inc(S["s_later"], 1)
                    if b == 3:
                        pe.wait_ge(S["s_masked"], h + 1)
                        pe.wait_ge(S["chunk_read_act"], acts_up_to(C_SBV + 1))
                        T.matmul(PS[:, 6, 0:SEQ], v_sb[:, 0, h * DH:(h + 1) * DH], work[:, 0, 0:SEQ],
                                 start=True, stop=False)
                        T.matmul(PS[:, 6, P:SEQ], v_sb[:, 1, h * DH:(h + 1) * DH], work[:, 0, SEQ:384],
                                 start=False, stop=True).then_inc(S["s_out"], 1)
                products(u)


B_CHUNKS = {1, 3, 5, 7}


def acts_up_to(c):
    return sum(1 for n in range(c + 1) if n not in BY_DVE and n not in B_CHUNKS)


def dve_reads(c):
    if C_OUT <= c < C_K:
        return "x1_ready", c - C_OUT + 1
    if C_OUTB <= c < C_CQ:
        return "x2_ready", c - C_OUTB + 1
    if c >= C_OUT2:
        return "y_scaled", c - C_OUT2 + 1
    return "chunk_read_dve", c - C_K + 1 if c < C_V else c - C_Q + 5


def scale_output(nc, S, dve, c, j, chunk_bank, yw, post_gain):
    if j == 0:
        dve.wait_ge(S["post_gain_loaded"], 16)
    dve.wait_ge(S["y_squared"], j + 1)
    for tok in range(TT):
        ins = nc.vector.tensor_tensor(yw[:, tok, j * NC:(j + 1) * NC], chunk_bank(c, tok),
                                      post_gain[:, j * NC:(j + 1) * NC], ALU.mult)
    ins.then_inc(S["y_scaled"], 1)


_INS = ["x", "a_norm_g", "a_w_in", "a_dw_w", "a_dw_b", "a_ln_g", "a_ln_b", "a_w_out", "kv_norm_g", "w_kv",
        "k_norm_g", "b_norm_g", "b_w_in", "b_q_norm_g", "b_lambda", "b_subln_g", "b_w_out", "positions_2",
        "pre_norm_w_2", "w_in_2", "q_norm_w_2", "w_q_up_2", "kv_norm_w_2", "w_kv_up_2", "w_out_2",
        "post_norm_w_2"]


def kernel(**inputs):
    import numpy as _np
    import concourse.bacc as _bacc
    from concourse import mybir as _mybir
    from concourse.bass_utils import run_bass_kernel_spmd as _run

    nc = _bacc.Bacc("TRN2", target_bir_lowering=False, num_devices=1)
    arrays, tensors = {}, {}
    for name in _INS:
        a = _np.ascontiguousarray(inputs[name])
        if name == "w_kv":
            a = a.reshape(1, *a.shape)
        arrays[f"in_{name}"] = a
        tensors[name] = nc.dram_tensor(f"in_{name}", a.shape, _mybir.dt.from_np(a.dtype),
                                       kind="ExternalInput").ap()
    out = nc.dram_tensor("out_y", (1, SEQ, D), _mybir.dt.float32, kind="ExternalOutput").ap()
    hybrid_program(nc, tensors, out)
    r = _run(nc, [arrays], core_ids=[0])
    return r.results[0]["out_y"]
```

```python
import math

import numpy as np

import concourse.bass as bass
from concourse import mybir
from contextlib import ExitStack

F32 = mybir.dt.float32
F32R = mybir.dt.float32r
ACT = mybir.ActivationFunctionType
ALU = mybir.AluOpType
AX = mybir.AxisListType

P = 128
SEQ = 256
TT = SEQ // P
D = 2048
KT = D // P
NC = 512
TAPS = 31
PAD = TAPS - 1
EPS = 1e-6
DH = 128
ROT = 64
HEADS = 8
LAM_INIT = 0.8 - 0.6 * math.exp(-0.3 * (2 - 1))
MASKED = -2.0 ** 100
ROPE_THETA = 10000.0

UP = list(range(KT))
CHUNKS = []
for j in range(4):
    CHUNKS += [("a_w_in", j * NC, NC, UP, "A", 0), ("a_w_in", D + j * NC, NC, UP, "A", 0)]
CHUNKS += [("a_w_in", 2 * D + j * NC, NC, UP, "A", 0) for j in range(4)]
CHUNKS += [("a_w_out", j * NC, NC, UP, "B", 0) for j in range(4)]
CHUNKS += [("w_kv", j * NC, NC, UP, "A", 0) for j in range(8)]
CHUNKS += [("b_w_in", j * NC, NC, UP, "B", 0) for j in range(8)]
CHUNKS += [("b_w_out", j * NC, NC, UP, "A", 0) for j in range(4)]
IN2 = dict(sb_q=0, sb_k=1024, sb_v=2048, sb_gate=3072, c_q=4096, c_kv=4608, mla_gate=4928)
CHUNKS += [("w_in_2", IN2["c_q"], 512, UP, "B", 0), ("w_in_2", IN2["c_kv"], 320, UP, "B", 0)]
CHUNKS += [("w_q_up_2", j * 384, 384, UP[:4], "A", 0) for j in range(4)]
CHUNKS += [("w_kv_up_2", j * NC, NC, UP[:2], "A", 4) for j in range(4)]
for part in ("sb_q", "sb_k", "sb_v", "mla_gate", "sb_gate"):
    CHUNKS += [("w_in_2", IN2[part] + j * NC, NC, UP, "B", 0) for j in range(2)]
CHUNKS += [("w_out_2", j * NC, NC, UP[8:] + UP[:8], "A", 0) for j in range(4)]
C_Z, C_OUT, C_K, C_V, C_Q, C_ZB, C_OUTB = 8, 12, 16, 20, 24, 28, 32
C_CQ, C_CKV, C_QUP, C_KVUP, C_SBQ, C_SBK, C_SBV, C_MG, C_SG, C_OUT2 = 36, 37, 38, 42, 46, 48, 50, 52, 54, 56
NCH = len(CHUNKS)

UNITS = [(c, i) for c in range(NCH) for i in range(len(CHUNKS[c][3]) // 2)]
FIRST = [next(u for u, (c, _) in enumerate(UNITS) if c == n) for n in range(NCH)] + [len(UNITS)]
NU = len(UNITS)
RAW, PARTS = 4, 3
AHEAD = PARTS - 1
CONV_FROM = [20, 36, 52, 68]
CONV_SLOTS = 16
CONV_WHOLE = set(range(CONV_SLOTS)) - {2, 5, 7, 10, 12, 15}
NORM_WHOLE = (91, 94)
WHOLE = [u in NORM_WHOLE or any(u - f - AHEAD in CONV_WHOLE for f in CONV_FROM) for u in range(NU)]
WINDOW_OPS = []
for tap in range(TAPS):
    if tap % 3:
        WINDOW_OPS += [("add", tap, i, 1.5) for i in (0, 2)]
    else:
        WINDOW_OPS += [("first" if tap == 0 else "tap", tap, i, 1.0) for i in range(4)]
PRODUCT_TAPS = [tap for tap in range(TAPS) if tap % 3]
CONV_OPS, PRODUCTS_AT = {}, {}
for j, f in enumerate(CONV_FROM):
    room = [8.5 if WHOLE[f + i + AHEAD] else 3.6 for i in range(CONV_SLOTS)]
    share = sum(op[3] for op in WINDOW_OPS) / sum(room)
    at, used, todo, added = 0.0, 0.0, list(WINDOW_OPS), []
    for i in range(CONV_SLOTS):
        at += room[i] * share
        CONV_OPS[f + i] = []
        while todo and (used < at or i == CONV_SLOTS - 1):
            op = todo.pop(0)
            used += op[3]
            CONV_OPS[f + i].append((j,) + op[:3])
            if op[0] == "add" and op[2] == 2:
                added.append(i)
    for m, i in enumerate(added):
        slot = f + max(i - 1, added[m - 2] if m >= 2 else 0, 0)
        PRODUCTS_AT.setdefault(slot, []).append((j, m, PRODUCT_TAPS[m]))
STATS_AT = [f + CONV_SLOTS + 1 for f in CONV_FROM]
MOMENTS_AT = STATS_AT[3] + 1
NORM_AT = [89, 91, 93, 95]
Z_EVAC_AT = [73, 80, 93, 96]
Z_AT = [92, 94, 97, 100]
SPLITS = []
SPLIT_NO = {}
for u in range(NU):
    if not WHOLE[u]:
        SPLIT_NO[u] = len(SPLITS)
        SPLITS.append(u)

DIFF_FROM, DIFF_STEP = FIRST[C_ZB] - 8, 5
MLA_FROM, MLA_STEP = FIRST[C_SBQ] + 3, 5
SB_FROM, SB_STEP = FIRST[C_MG], 4
Z2_AT = [FIRST[C_ZB] + at for at in (9, 19, 24, 32)]
GATE_AT = [FIRST[C_ZB] + at for at in (10, 20, 25, 34)]
OG_AT = [at + 2 for at in GATE_AT]
QU_AT = [FIRST[C_QUP + 2] + 1, FIRST[C_QUP + 2] + 2, FIRST[C_QUP + 3] + 2, FIRST[C_KVUP] + 1]
HG_AT = {"mg": [FIRST[C_MG + 1] + 5, FIRST[C_SG] + 5], "sg": [FIRST[C_SG + 1] + 5, FIRST[C_OUT2] + 4]}

EVENTS = [(f"x{j}", "whole") for j in range(4)] + [(f"y{j}", "copy") for j in range(4)]
EVENTS += [(f"z{j}", "mul") for j in range(4)] + [(f"w{j}", "lo") for j in range(4)]
for j in range(4):
    EVENTS += [(f"b{j}", "kept"), (f"k{j}", "copy")]
EVENTS += [(f"q{j}", "copy") for j in range(4)] + [(f"og{j}", "lo") for j in range(4)]
EVENTS += [(f"v{j}", "lo") for j in range(4)] + [("cq", "lo"), ("ckv", "lo")]
EVENTS += [(f"qu{j}", "copy") for j in range(4)] + [(f"ku{j}", "copy") for j in range(4)]
EVENTS += [(f"{m}{j}", "copy") for m in ("sq", "sk") for j in range(2)]
EVENTS += [(f"{m}{j}", "mul") for m in ("mg", "sg") for j in range(2)]
X_AT = [None, 1, 3, 5]
T_EVENTS = [(n, k) for n, k in EVENTS if k != "kept"]
T_NO = {n: i for i, (n, _) in enumerate(T_EVENTS)}
LO_NO = {n: i for i, n in enumerate([n for n, k in EVENTS if k != "copy"])}
MUL_NO = {n: i for i, n in enumerate([n for n, k in EVENTS if k == "mul"])}
COPY_NO = {n: i for i, n in enumerate([n for n, k in EVENTS if k == "copy"])}

RS = [("x", 2), ("ln", 2), ("x1", 2)] + [(f"k{j}", 8) for j in range(4)] + [(f"q{j}", 8) for j in range(3)]
RS += [("o0", 2), ("q3", 8)] + [(f"o{h}", 2) for h in range(1, HEADS)] + [("x2", 2), ("cq", 2), ("ckv", 2), ("post", 2)]
RS_NO = {n: i for i, (n, _) in enumerate(RS)}
SS_NO = {n: i for i, n in enumerate([n for n, _ in RS if n not in ("x", "ln")])}

BY_DVE = set(range(C_OUT, C_V)) | set(range(C_Q, C_ZB)) | set(range(C_OUTB, C_CQ)) | set(range(C_OUT2, NCH))

ROWS = {}
for name, n in (("a_norm_g", 16), ("a_ln_g", 16), ("a_ln_b", 16), ("a_dw_b", 16), ("kv_norm_g", 16),
                ("b_norm_g", 16), ("pre_norm_w_2", 16), ("k_norm_g", 1), ("b_q_norm_g", 1),
                ("b_subln_g", 2), ("q_norm_w_2", 4), ("kv_norm_w_2", 2)):
    ROWS[name] = (sum(k for _, k in ROWS.values()), n)
NROWS = sum(k for _, k in ROWS.values())

PI_A = 6.28125
PI_B = float(np.float32(np.round((2 * math.pi - PI_A) * 2 ** 20) / 2 ** 20))
PI_C = 2 * math.pi - PI_A - PI_B
ROUND = 12582912.0
PI_LOW = 3.1415925

SEMS = """x0_loaded x1_loaded x2_loaded x3_loaded gain_loaded rows_loaded post_gain_loaded out_stored
w0_loaded w1_loaded w2_loaded w3_loaded consts_ready
units_done t_full gain_full gain_ready tables_full x_first_lo x_whole
w_hi_ready t_hi_ready t_copied chunk_read_act x_squared sumsq_ready guess_ready act_chain
w_lo_ready t_multiplied lo_ready chunk_read_dve var_ready dve_chain
tables_ready x_scale_ready sig_ready y_ready product_ready product_added conv_ready stats_full stats_read diag_ready
moments_full moments_ready normed silu_ready x1_ready x1_kept x1_scale_ready x2_ready x2_scale_ready
lam_in lam_exp angle_ready sines_ready 
on_ready
d_scores d_negmax d_exp d_probs d_pt d_pt_copied d_out d_gated
cq_scaled ckv_scaled kr_staged kr_roped qu_roped 
m_scores m_negmax m_exp m_probs m_pt m_pt_copied m_out m_out_copied
s_scores s_soft s_keep s_later s_logit s_weight s_masked s_out s_out_copied
y_scaled y_squared last_scaled final_ready""".split()


def hybrid_program(nc, t, out):
    with ExitStack() as ctx:
        def sb(name, shape, dt=F32):
            return ctx.enter_context(nc.sbuf_tensor(name, shape, dt))

        S = {n: ctx.enter_context(nc.semaphore(n)) for n in SEMS}

        x_res = sb("x_res", [P, TT, D])
        hi = {"A": sb("actA_hi", [P, KT, SEQ], F32R), "B": sb("actB_hi", [P, KT, SEQ], F32R)}
        lo = {"A": sb("actA_lo", [P, KT, SEQ], F32R), "B": sb("actB_lo", [P, KT, SEQ], F32R)}
        w_raw = sb("w_raw", [P, RAW, 2 * NC])
        w_hi = sb("w_hi", [P, PARTS, 2 * NC], F32R)
        w_lo = sb("w_lo", [P, PARTS, 2 * NC], F32R)
        stage = sb("stage", [P, 2, TT, NC])
        heads_out = sb("heads_out", [P, 4, TT, 2 * DH])
        work = sb("work", [P, 2, 384])
        probs_t = sb("probs_t", [P, 384])
        ident = sb("ident", [P, P])
        strict = sb("strict", [P, P])
        after = sb("after", [P, P])
        ones = sb("ones", [P, P])
        neg_ones = sb("neg_ones", [P, P])
        mask_row = sb("mask_row", [1, 2 * P], mybir.dt.bfloat16)
        gains = sb("gains", [P, NROWS + 6])
        st = sb("st", [P, 1024])
        rope = sb("rope", [P, 8, TT, 32])
        pos_i = sb("pos_i", [P, TT], mybir.dt.int32)
        aux = sb("aux", [P, 14592])
        PS = ctx.enter_context(nc.psum_tensor("PS", [P, 8, NC], F32))

        def view(at, *shape):
            n = int(np.prod(shape))
            a = aux[:, at:at + n]
            if len(shape) == 3:
                return a.rearrange("p (a b c) -> p a b c", a=shape[0], b=shape[1])
            return a.rearrange("p (a b) -> p a b", a=shape[0]) if len(shape) == 2 else a

        y_pad = view(0, KT, PAD + SEQ)
        conv = view(KT * (PAD + SEQ), KT, SEQ)
        x_t = view(KT * (PAD + 2 * SEQ), KT, SEQ)
        taps = view(KT * (PAD + 3 * SEQ), KT, TAPS)
        moments = view(KT * (PAD + 3 * SEQ + TAPS), 2, SEQ)
        diag = view(KT * (PAD + 3 * SEQ + TAPS) + 2 * SEQ, 4, P)
        k_t = view(0, KT, SEQ)
        q_t = view(KT * SEQ, KT, SEQ)
        vals = view(2 * KT * SEQ, TT, D)
        x1_t = q_t
        o_squares = view(3 * KT * SEQ, TT, 2 * DH)
        H8 = HEADS * SEQ
        qn_t, kn_t, qr_t = view(0, HEADS, SEQ), view(H8, HEADS, SEQ), view(2 * H8, HEADS, SEQ)
        v_mla, sq_t, sk_t = view(3 * H8, TT, HEADS * DH), view(4 * H8, HEADS, SEQ), view(5 * H8, HEADS, SEQ)
        v_sb, kr_t = view(6 * H8, TT, HEADS * DH), view(7 * H8, SEQ)
        yw = view(0, TT, D)
        post_gain = aux[:, 2 * H8:3 * H8]
        qu_stage = heads_out[:, :, :, :].rearrange("p a b c -> p (a b c)")[:, 0:4 * 384]\
            .rearrange("p (i t n) -> p i t n", i=2, t=TT)
        junk = heads_out[:, :, :, :].rearrange("p a b c -> p (a b c)")

        cursor = [0]

        def small(n):
            cursor[0] += n
            return st[:, cursor[0] - n:cursor[0]]

        root = {n: dict(ss=small(k), v=small(k), ln=small(k), y=small(k), t=small(k), r=small(k))
                for n, k in RS}
        k_scale = {f"{m}{j}": small(8) for m in "kq" for j in range(4)}
        cq_scale, ckv_scale = small(2), small(2)
        qk_gain, sub_gain = small(1), small(2)
        lam_sums, lam_exps, neg_lam = small(2), small(2), small(1)
        bn = small(2 * 4 * 6)
        mv = small(4)
        y_sums = small(8)
        neg_max, sums, recips, neg_r = small(4), small(4), small(4), small(2)
        pos_f = small(2)

        def gain(name, i):
            r, _ = ROWS[name]
            return gains[:, r + i:r + i + 1]

        def act_hi(which, k):
            return hi[which][:, k, :]

        def chunk_bank(c, tok, w=None):
            return PS[:, 2 * (c % 2) + tok, 0:(w or CHUNKS[c][2])]

        def w_view(ring, slot, w):
            return ring[:, slot, 0:2 * w].rearrange("p (k n) -> p k n", k=2)

        def bank_pair(i):
            return PS[:, 4 + i, :].rearrange("p (c s) -> p c s", c=2)

        def sb_weight(h):
            return junk[:, 384 * (h % 2):384 * (h % 2) + 384]

        def product(n):
            return junk[:, 1024 * (n % 2):1024 * (n % 2) + 1024].rearrange("p (k s) -> p k s", k=4)

        def chunk_done(eng, c):
            eng.wait_ge(S["units_done"], FIRST[c + 1])

        def transposed(eng, name):
            eng.wait_ge(S["t_full"], T_NO[name] + 1)

        block = ctx.enter_context(nc.Block())

        @block.sync
        def _(sp):
            def load_x(j):
                sp.dma_start(x_res[:, :, j * NC:(j + 1) * NC],
                             t["x"][0, :, j * NC:(j + 1) * NC].rearrange("(t p) n -> p t n", p=P))\
                    .then_inc(S[f"x{j}_loaded"], 16)

            n_rows = [0]

            def load_rows(dst, src):
                n_rows[0] += 16
                sp.dma_start(dst, src).then_inc(S["rows_loaded"], 16)

            def load_small():
                for name, (r, n) in ROWS.items():
                    if name == "a_norm_g":
                        continue
                    src = t[name]
                    src = src[0, :] if len(src.shape) == 2 else src
                    load_rows(stage[r:r + n, 0, 0, 0:P], src.rearrange("(r c) -> r c", c=P))
                load_rows(junk[0:TAPS, 0:D], t["a_dw_w"][0, :, :])
                load_rows(work[:, :, :].rearrange("p a b -> p (a b)")[:, 0:4 * DH],
                          t["b_lambda"].rearrange("o a d -> o (a d)").to_broadcast([P, 4 * DH]))
                with nc.allow_non_contiguous_dma(reason="256 positions, one to a partition and token tile"):
                    load_rows(pos_i[:, :], t["positions_2"][0, :].rearrange("(t p) -> p t", p=P))
                assert n_rows[0] == 16 * 14

            load_x(0)
            for u, (c, i) in enumerate(UNITS):
                name, col, w, kts, _, _ = CHUNKS[c]
                if u in (2, 3, 4):
                    load_x(u - 1)
                if u == 4:
                    load_small()
                if u >= RAW:
                    if WHOLE[u - RAW]:
                        sp.wait_ge(S["units_done"], u - RAW + 1)
                    else:
                        sp.wait_ge(S["w_lo_ready"], SPLIT_NO[u - RAW] + 1)
                k = kts[2 * i]
                sp.dma_start(w_view(w_raw, u % RAW, w),
                             t[name].rearrange("o (k p) n -> (o k) p n", p=P)[k:k + 2, :, col:col + w]
                             .rearrange("k p n -> p k n")).then_inc(S[f"w{u % RAW}_loaded"], 16)
                if u == FIRST[C_SG]:
                    sp.wait_ge(S["m_out"], HEADS)
                    sp.dma_start(post_gain, t["post_norm_w_2"][0:1, :].to_broadcast([P, D]))\
                        .then_inc(S["post_gain_loaded"], 16)
            for i in range(8):
                sp.wait_ge(S["final_ready"], i + 1)
                tok, j = i % 2, i // 2
                sp.dma_start(out[0, tok * P:(tok + 1) * P, j * NC:(j + 1) * NC],
                             yw[:, tok, j * NC:(j + 1) * NC]).then_inc(S["out_stored"], 16)
            sp.wait_ge(S["out_stored"], 8 * 16)

        @block.gpsimd
        def _(pool):
            chain = nc.gpsimd
            chain.memset(ident[:, :], 0.0)
            chain.memset(strict[:, :], 1.0)
            chain.memset(after[:, :], -1.0)
            chain.memset(ones[:, :], 1.0)
            chain.memset(neg_ones[:, :], -1.0)
            chain.memset(mask_row[:, 0:64], 1.0)
            chain.memset(mask_row[:, 64:P + 64], 0.0)
            chain.memset(mask_row[:, P + 64:2 * P], MASKED)
            chain.memset(y_pad[:, :, 0:PAD], 0.0)
            inv_freq = np.float32(ROPE_THETA) ** (-np.arange(0, ROT, 2, dtype=np.float32) / np.float32(ROT))
            for i in range(ROT // 2):
                last = chain.memset(rope[:, 7, 0, i:i + 1], float(inv_freq[i]))
            last.then_inc(S["consts_ready"], 1)
            pool.wait_ge(S["consts_ready"], 1)
            chain.affine_select(out=ident[:, :], in_=ident[:, :], compare_op=ALU.not_equal, fill=1.0,
                                base=0, pattern=[[-1, P]], channel_multiplier=1)
            chain.affine_select(out=strict[:, :], in_=strict[:, :], compare_op=ALU.is_gt, fill=0.0,
                                base=0, pattern=[[1, P]], channel_multiplier=-1)
            chain.affine_select(out=after[:, :], in_=after[:, :], compare_op=ALU.is_gt, fill=0.0,
                                base=0, pattern=[[-1, P]], channel_multiplier=1).then_inc(S["consts_ready"], 1)

        @block.scalar
        def _(act):
            n_chain = [0]

            def link(ins):
                n_chain[0] += 1
                ins.then_inc(S["act_chain"], 1)
                act.wait_ge(S["act_chain"], n_chain[0])

            EXP_LN, SILU, SIGMOID = "natural_log_exp_and_others", "silu_and_others", "sigmoid_and_others"
            table = [None]

            def want(name):
                if table[0] != name:
                    nc.scalar.preload_act_table_set(name)
                    table[0] = name

            act.dma_start(stage[0:KT, 0, 0, 0:P], t["a_norm_g"][0, :].rearrange("(r c) -> r c", c=P))\
                .then_inc(S["gain_loaded"], 16)
            def split(u):
                if u >= NU or WHOLE[u]:
                    return
                n, w = SPLIT_NO[u], CHUNKS[UNITS[u][0]][2]
                act.wait_ge(S[f"w{u % RAW}_loaded"], 16 * (u // RAW + 1))
                if n >= PARTS:
                    act.wait_ge(S["units_done"], SPLITS[n - PARTS] + 1)
                nc.scalar.activation(w_hi[:, n % PARTS, 0:2 * w], w_raw[:, u % RAW, 0:2 * w], ACT.Copy)\
                    .then_inc(S["w_hi_ready"], 1)

            def hi_parts(name, which, k0, gain_name, tiles=range(4)):
                transposed(act, name)
                for i in tiles:
                    g = gain(gain_name, k0 + i)
                    ins = nc.scalar.activation(act_hi(which, k0 + i), bank_pair(i // 2)[:, i % 2, :],
                                               ACT.Copy, scale=g)
                    if i % 2:
                        ins.then_inc(S["t_hi_ready"], 1)

            def guess(name):
                want(EXP_LN)
                act.wait_ge(S["var_ready"], RS_NO[name] + 1)
                link(nc.scalar.activation(root[name]["ln"], root[name]["v"], ACT.Ln))
                nc.scalar.activation(root[name]["y"], root[name]["ln"], ACT.Exp, scale=-0.5)\
                    .then_inc(S["guess_ready"], 1)

            def squares_of_rows(name, tok):
                ins = nc.scalar.activation(junk, x_res[:, tok, :], ACT.Square,
                                           accum_out=root[name]["ss"][:, tok:tok + 1])
                if tok == 0:
                    link(ins)
                else:
                    ins.then_inc(S["sumsq_ready"], 1)

            def squares_of_chunk(c, w, name, scale):
                for tok in range(TT):
                    ins = nc.scalar.activation(work[:, :, :].rearrange("p a b -> p (a b)")[:, 0:w],
                                               chunk_bank(c, tok, w), ACT.Square,
                                               scale=scale[:, tok:tok + 1],
                                               accum_out=root[name]["ss"][:, tok:tok + 1])
                    if tok == 0:
                        link(ins)
                ins.then_inc(S["sumsq_ready"], 1)

            def squares_of_output(c, j):
                for tok in range(TT):
                    if c == NCH - 1 and tok == 1:
                        act.wait_ge(S["last_scaled"], 1)
                    nc.scalar.activation(junk[:, tok * NC:(tok + 1) * NC],
                                         chunk_bank(c, tok), ACT.Square,
                                         accum_out=y_sums[:, 4 * tok + j:4 * tok + j + 1])\
                        .then_inc(S["y_squared"], 1)

            def evacuate(c, dst, func, scale, w=None, last=True):
                if func in (ACT.Silu, ACT.Sigmoid):
                    want(SILU if func == ACT.Silu else SIGMOID)
                chunk_done(act, c)
                for tok in range(TT):
                    ins = nc.scalar.activation(dst(tok), chunk_bank(c, tok, w), func,
                                               scale=1.0 if scale is None else scale[:, tok:tok + 1])
                if last:
                    ins.then_inc(S["chunk_read_act"], 1)
                return ins

            def copy_pairs(name, dst, scale, n=2):
                transposed(act, name)
                for i in range(n):
                    ins = nc.scalar.activation(dst(i), bank_pair(i), ACT.Copy, scale=scale)
                ins.then_inc(S["t_copied"], 1)

            def stage_at(i):
                return lambda tok: stage[:, i, tok, :]

            r_x, r_x1, r_x2 = root["x"]["r"], root["x1"]["r"], root["x2"]["r"]

            want(EXP_LN)
            act.wait_ge(S["gain_full"], 1)
            nc.scalar.activation(gains[:, 0:KT], PS[:, 6, 0:KT], ACT.Copy).then_inc(S["gain_ready"], 1)
            act.wait_ge(S["gain_ready"], 1)
            for u in range(AHEAD):
                hi_parts("x0", "A", 0, "a_norm_g", tiles=(2 * u, 2 * u + 1))
                split(u)
            for u, (c, s) in enumerate(UNITS):
                h, b = divmod(u - MLA_FROM, MLA_STEP)
                if 0 <= h < HEADS:
                    if b == 0:
                        act.wait_ge(S["m_negmax"], h + 1)
                        for tok, (f, e) in enumerate(((0, 128), (128, 384))):
                            ins = nc.scalar.activation(work[:, h % 2, f:e], PS[:, 6, f:e], ACT.Exp,
                                                       bias=neg_max[:, tok:tok + 1],
                                                       accum_out=sums[:, tok:tok + 1])
                        ins.then_inc(S["m_exp"], 1)
                    if b == 2:
                        act.wait_ge(S["m_pt"], h + 1)
                        nc.scalar.activation(probs_t[:, :], PS[:, 7, 0:384], ACT.Copy)\
                            .then_inc(S["m_pt_copied"], 1)
                    if b == 3:
                        act.wait_ge(S["m_out"], h + 1)
                        nc.scalar.activation(qn_t[:, h, :], PS[:, 6, 0:SEQ], ACT.Copy)\
                            .then_inc(S["m_out_copied"], 1)
                h, b = divmod(u - DIFF_FROM, DIFF_STEP)
                if 0 <= h < HEADS:
                    if b == 3:
                        act.wait_ge(S["d_pt"], h + 1)
                        nc.scalar.activation(probs_t[:, :], PS[:, 6, 0:384], ACT.Copy)\
                            .then_inc(S["d_pt_copied"], 1)
                split(u + AHEAD)
                if u in X_AT:
                    j = X_AT.index(u)
                    hi_parts(f"x{j}", "A", 4 * j, "a_norm_g")
                if u == 4:
                    act.wait_ge(S["tables_full"], 1)
                    nc.scalar.activation(gains[:, KT:NROWS], PS[:, 6, KT:NROWS], ACT.Copy)
                    nc.scalar.activation(taps.rearrange("p a b -> p (a b)"), PS[:, 7, 0:KT * TAPS], ACT.Copy)\
                        .then_inc(S["tables_ready"], 1)
                    act.wait_ge(S["tables_ready"], 1)
                if u in (2, 4):
                    tok = u // 2 - 1
                    for j in range(4 if u == 2 else 0):
                        act.wait_ge(S[f"x{j}_loaded"], 16)
                    nc.scalar.activation(conv[:, 8 * tok:8 * tok + 8, :].rearrange("p a b -> p (a b)"),
                                         x_res[:, tok, :], ACT.Square,
                                         accum_out=root["x"]["ss"][:, tok:tok + 1])\
                        .then_inc(S["x_squared"], 1)
                if u == 6:
                    guess("x")
                if u == 10:
                    act.wait_ge(S["lam_in"], 1)
                    nc.scalar.activation(lam_exps, lam_sums, ACT.Exp).then_inc(S["lam_exp"], 1)
                    act.wait_ge(S["angle_ready"], 1)
                    nc.scalar.activation(rope[:, 2, :, :], rope[:, 0, :, :], ACT.Sin)
                    nc.scalar.activation(rope[:, 3, :, :], rope[:, 0, :, :], ACT.Sin, scale=0.5)\
                        .then_inc(S["sines_ready"], 1)
                    want(SIGMOID)
                if s == 0 and 1 <= c <= C_Z and c % 2:
                    j = c // 2
                    act.wait_ge(S["x_scale_ready"], 1)
                    if j:
                        act.wait_ge(S["y_ready"], j)
                    evacuate(c - 1, stage_at(0), ACT.Copy, r_x)
                if s == 0 and 1 <= c <= C_Z and c % 2 == 0:
                    j = c // 2 - 1
                    if j:
                        transposed(act, f"y{j - 1}")
                    ins = evacuate(c - 1, stage_at(1), ACT.Sigmoid, r_x, last=False)
                    ins.then_inc(S["sig_ready"], 1)
                if s == 3 and 2 <= c <= C_Z and c % 2 == 0:
                    j = c // 2 - 1
                    copy_pairs(f"y{j}", lambda i: y_pad[:, 4 * j + 2 * i:4 * j + 2 * i + 2, PAD:PAD + SEQ], 1.0)
                if u == MOMENTS_AT:
                    guess("ln")
                if u == MOMENTS_AT + 2:
                    act.wait_ge(S["moments_full"], 1)
                    nc.scalar.activation(moments.rearrange("p a b -> p (a b)"), PS[:, 6, :], ACT.Copy)\
                        .then_inc(S["moments_ready"], 1)
                if u - 1 in NORM_AT:
                    j = NORM_AT.index(u - 1)
                    want(SILU)
                    act.wait_ge(S["normed"], j + 1)
                    for k in range(4 * j, 4 * j + 4):
                        ins = nc.scalar.activation(conv[:, k, :], conv[:, k, :], ACT.Silu,
                                                   scale=gain("a_ln_g", k), bias=gain("a_ln_b", k))
                    ins.then_inc(S["silu_ready"], 1)
                if u in Z_EVAC_AT:
                    j = Z_EVAC_AT.index(u)
                    if j == 0:
                        act.wait_ge(S["y_ready"], 4)
                    if j == 1:
                        transposed(act, "y3")
                    if j >= 2:
                        transposed(act, f"z{j - 2}")
                    evacuate(C_Z + j, stage_at(j % 2), ACT.Silu, r_x)
                if u in Z_AT:
                    j = Z_AT.index(u)
                    for i in range(2):
                        act.wait_ge(S["t_multiplied"], MUL_NO[f"z{j}"] * 2 + i + 1)
                        ins = nc.scalar.activation(hi["B"][:, 4 * j + 2 * i:4 * j + 2 * i + 2, :],
                                                   conv[:, 4 * j + 2 * i:4 * j + 2 * i + 2, :], ACT.Copy)
                        ins.then_inc(S["t_hi_ready"], 1)
                if s == 2 and C_OUT < c <= C_K:
                    j = c - C_OUT - 1
                    transposed(act, f"w{j}")
                    for i in range(2):
                        ins = nc.scalar.activation(x1_t[:, 4 * j + 2 * i:4 * j + 2 * i + 2, :], bank_pair(i),
                                                   ACT.Copy)
                    ins.then_inc(S["x1_kept"], 1)
                    hi_parts(f"w{j}", "A", 4 * j, "kv_norm_g")
                if u == FIRST[C_K] + 2:
                    act.wait_ge(S["x1_ready"], 4)
                    squares_of_rows("x1", 0)
                if u == FIRST[C_K] + 5:
                    squares_of_rows("x1", 1)
                if u == FIRST[C_K] + 6:
                    guess("x1")
                if s == 4 and C_K <= c < C_V:
                    j = c - C_K
                    act.wait_ge(S["x1_kept"], j + 1)
                    for k in range(4 * j, 4 * j + 4):
                        ins = nc.scalar.activation(act_hi("B", k), x1_t[:, k, :], ACT.Copy,
                                                   scale=gain("b_norm_g", k))
                        if k % 2:
                            ins.then_inc(S["t_hi_ready"], 1)
                for m, c0, dst, scale in (("k", C_K, k_t, 1.0), ("q", C_Q, q_t, qk_gain)):
                    if s == 0 and c0 < c <= c0 + 4:
                        j = c - c0 - 1
                        chunk_done(act, c - 1)
                        if j >= 2:
                            transposed(act, f"{m}{j - 2}")
                        elif m == "k" and j == 0:
                            transposed(act, "z3")
                            act.wait_ge(S["x1_scale_ready"], 1)
                        elif m == "q":
                            transposed(act, f"k{j + 2}")
                        for tok in range(TT):
                            ins = nc.scalar.activation(stage[:, j % 2, tok, :], chunk_bank(c - 1, tok),
                                                       ACT.Square, scale=r_x1[:, tok:tok + 1])
                        ins.then_inc(S["sumsq_ready"], 1)
                    if s == 1 and c0 < c <= c0 + 4:
                        guess(f"{m}{c - c0 - 1}")
                    if s == 3 and c0 < c <= c0 + 4:
                        j = c - c0 - 1
                        copy_pairs(f"{m}{j}", lambda i: dst[:, 4 * j + 2 * i:4 * j + 2 * i + 2, :], scale)
                if s == 0 and C_V < c <= C_V + 4:
                    j = c - C_V - 1
                    evacuate(c - 1, lambda tok: vals[:, tok, j * NC:(j + 1) * NC], ACT.Copy, r_x1)
                h, b = divmod(u - DIFF_FROM, DIFF_STEP)
                if 0 <= h < HEADS:
                    if b == 1:
                        want(EXP_LN)
                        act.wait_ge(S["d_negmax"], h + 1)
                        for m in range(2):
                            for tok, (f, e) in enumerate(((0, 128), (128, 384))):
                                i = 2 * m + tok
                                ins = nc.scalar.activation(work[:, m, f:e], PS[:, 6 + m, f:e], ACT.Exp,
                                                           bias=neg_max[:, i:i + 1],
                                                           accum_out=sums[:, i:i + 1])
                        ins.then_inc(S["d_exp"], 1)
                h, b = divmod(u - DIFF_FROM - DIFF_STEP, DIFF_STEP)
                if 0 <= h < HEADS and b == 0:
                    act.wait_ge(S["on_ready"], h + 1)
                    for tok in range(TT):
                        ins = nc.scalar.activation(o_squares[:, tok, :], heads_out[:, h % 4, tok, :],
                                                   ACT.Square, accum_out=root[f"o{h}"]["ss"][:, tok:tok + 1])
                    ins.then_inc(S["sumsq_ready"], 1)
                if 0 <= h < HEADS and b == 1:
                    guess(f"o{h}")
                if u in Z2_AT:
                    j = Z2_AT.index(u)
                    if j < 2:
                        transposed(act, f"q{j + 2}")
                    else:
                        act.wait_ge(S["d_gated"], j - 1)
                    evacuate(C_ZB + j, stage_at(j % 2), ACT.Silu, r_x1)
                    want(EXP_LN)
                if u in OG_AT:
                    j = OG_AT.index(u)
                    transposed(act, f"og{j}")
                    for i in range(4):
                        ins = nc.scalar.activation(act_hi("A", 4 * j + i), bank_pair(i // 2)[:, i % 2, :],
                                                   ACT.Copy, scale=sub_gain[:, i % 2:i % 2 + 1])
                        if i % 2:
                            ins.then_inc(S["t_hi_ready"], 1)
                if s == 2 and C_OUTB < c <= C_CQ:
                    j = c - C_OUTB - 1
                    hi_parts(f"v{j}", "B", 4 * j, "pre_norm_w_2")
                if u == FIRST[C_CQ] + 2:
                    act.wait_ge(S["x2_ready"], 4)
                    squares_of_rows("x2", 0)
                if u == FIRST[C_CQ] + 5:
                    squares_of_rows("x2", 1)
                if u == FIRST[C_CQ] + 6:
                    guess("x2")
                if u == FIRST[C_CKV]:
                    chunk_done(act, C_CQ)
                    act.wait_ge(S["x2_scale_ready"], 1)
                    squares_of_chunk(C_CQ, 512, "cq", r_x2)
                    evacuate(C_CQ, stage_at(0), ACT.Copy, None)
                if u == FIRST[C_CKV] + 1:
                    guess("cq")
                if u == FIRST[C_CKV] + 4:
                    hi_parts("cq", "A", 0, "q_norm_w_2")
                if u == FIRST[C_QUP]:
                    chunk_done(act, C_CKV)
                    squares_of_chunk(C_CKV, 256, "ckv", r_x2)
                    for tok in range(TT):
                        ins = nc.scalar.activation(stage[:, 1, tok, 256:320],
                                                   PS[:, 2 * (C_CKV % 2) + tok, 256:320], ACT.Copy,
                                                   scale=r_x2[:, tok:tok + 1])
                    ins.then_inc(S["kr_staged"], 1)
                    evacuate(C_CKV, lambda tok: stage[:, 1, tok, 0:256], ACT.Copy, None, w=256)
                if u == FIRST[C_QUP] + 1:
                    guess("ckv")
                if u == FIRST[C_QUP] + 2:
                    transposed(act, "ckv")
                    nc.scalar.activation(kr_t[0:ROT, :], PS[0:ROT, 5, 0:SEQ], ACT.Copy)
                    for i in range(2):
                        ins = nc.scalar.activation(act_hi("A", 4 + i), bank_pair(0)[:, i, :],
                                                   ACT.Copy, scale=gain("kv_norm_w_2", i))
                    ins.then_inc(S["t_hi_ready"], 1)
                if s == 0 and C_QUP < c <= C_KVUP:
                    j = c - C_QUP - 1
                    chunk_done(act, c - 1)
                    if j >= 2:
                        transposed(act, f"qu{j - 2}")
                    if j == 0:
                        act.wait_ge(S["cq_scaled"], 1)
                    for tok in range(TT):
                        ins = nc.scalar.activation(qu_stage[:, j % 2, tok, :], chunk_bank(c - 1, tok), ACT.Copy,
                                                   scale=cq_scale[:, tok:tok + 1])
                    ins.then_inc(S["chunk_read_act"], 1)
                for j in range(4):
                    if u == QU_AT[j]:
                        transposed(act, f"qu{j}")
                        nc.scalar.activation(qn_t[:, 2 * j:2 * j + 2, :], bank_pair(0), ACT.Copy,
                                             scale=float(192 ** -0.5))
                        nc.scalar.activation(qr_t[0:ROT, 2 * j:2 * j + 2, :], bank_pair(1)[0:ROT], ACT.Copy,
                                             scale=float(192 ** -0.5)).then_inc(S["t_copied"], 1)
                if s == 0 and C_KVUP < c <= C_SBQ:
                    j = c - C_KVUP - 1
                    chunk_done(act, c - 1)
                    if j == 0:
                        transposed(act, "cq")
                        act.wait_ge(S["ckv_scaled"], 1)
                    elif j == 1:
                        transposed(act, "ckv")
                    else:
                        transposed(act, f"ku{j - 2}")
                    for tok in range(TT):
                        kv = chunk_bank(c - 1, tok).rearrange("p (h m n) -> p h m n", h=2, m=2)
                        nc.scalar.activation(stage[:, j % 2, tok, 0:256].rearrange("p (h n) -> p h n", h=2),
                                             kv[:, :, 0, :], ACT.Copy, scale=ckv_scale[:, tok:tok + 1])
                        ins = nc.scalar.activation(v_mla[:, tok, 256 * j:256 * j + 256]
                                                   .rearrange("p (h n) -> p h n", h=2),
                                                   kv[:, :, 1, :], ACT.Copy, scale=ckv_scale[:, tok:tok + 1])
                    ins.then_inc(S["chunk_read_act"], 1)
                for j in range(4):
                    if u == FIRST[C_KVUP + j + 1] + 1:
                        copy_pairs(f"ku{j}", lambda i: kn_t[:, 2 * j:2 * j + 2, :], 1.0, n=1)
                for m, c0, dst, scale in (("sq", C_SBQ, sq_t, float(DH ** -0.5)), ("sk", C_SBK, sk_t, 1.0)):
                    if s == 0 and c0 < c <= c0 + 2:
                        j = c - c0 - 1
                        transposed(act, f"ku{j + 2}" if m == "sq" else f"sq{j}")
                        evacuate(c - 1, stage_at(j), ACT.Copy, r_x2)
                    if s == 2 and c0 < c <= c0 + 2:
                        j = c - c0 - 1
                        copy_pairs(f"{m}{j}", lambda i: dst[:, 4 * j + 2 * i:4 * j + 2 * i + 2, :], scale)
                if s == 0 and C_SBV < c <= C_SBV + 2:
                    j = c - C_SBV - 1
                    evacuate(c - 1, lambda tok: v_sb[:, tok, j * NC:(j + 1) * NC], ACT.Copy, r_x2)
                h, b = divmod(u - SB_FROM, SB_STEP)
                if 0 <= h < HEADS:
                    if b == 0:
                        act.wait_ge(S["s_scores"], h + 1)
                        link(nc.scalar.activation(work[:, 0, :], PS[:, 6, 0:384], ACT.Abs))
                        link(nc.scalar.activation(work[:, 0, :], work[:, 0, :], ACT.Exp, scale=-1.0))
                        nc.scalar.activation(work[:, 0, :], work[:, 0, :], ACT.Ln, bias=1.0)\
                            .then_inc(S["s_soft"], 1)
                    if b == 3:
                        act.wait_ge(S["s_logit"], h + 1)
                        if h >= 2:
                            act.wait_ge(S["s_out"], h - 1)
                        nc.scalar.activation(sb_weight(h), probs_t[:, :], ACT.Exp).then_inc(S["s_weight"], 1)
                h, b = divmod(u - SB_FROM - SB_STEP, SB_STEP)
                if 0 <= h < HEADS and b == 1:
                    act.wait_ge(S["s_out"], h + 1)
                    nc.scalar.activation(sq_t[:, h, :], PS[:, 7, 0:SEQ], ACT.Copy)\
                        .then_inc(S["s_out_copied"], 1)
                for m, c0, k0 in (("mg", C_MG, 8), ("sg", C_SG, 0)):
                    if s == 2 and c0 < c <= c0 + 2:
                        j = c - c0 - 1
                        transposed(act, f"sk{j}" if m == "mg" else f"mg{j}")
                        evacuate(c - 1, stage_at(j), ACT.Silu, r_x2)
                        want(EXP_LN)
                    if u in HG_AT[m]:
                        j = HG_AT[m].index(u)
                        gated = qn_t if m == "mg" else sq_t
                        for i in range(2):
                            act.wait_ge(S["t_multiplied"], MUL_NO[f"{m}{j}"] * 2 + i + 1)
                            nc.scalar.activation(hi["A"][:, k0 + 4 * j + 2 * i:k0 + 4 * j + 2 * i + 2, :],
                                                 gated[:, 4 * j + 2 * i:4 * j + 2 * i + 2, :], ACT.Copy)\
                                .then_inc(S["t_hi_ready"], 1)
                if s == 0 and c > C_OUT2:
                    j = c - C_OUT2 - 1
                    chunk_done(act, c - 1)
                    squares_of_output(c - 1, j)
                for j, m, tap in PRODUCTS_AT.get(u, []):
                    n = j * len(PRODUCT_TAPS) + m
                    act.wait_ge(S["t_copied"], COPY_NO[f"y{j}"] + 1)
                    if n >= 2:
                        act.wait_ge(S["product_added"], n - 1)
                    for k in range(4 * j, 4 * j + 4):
                        ins = nc.scalar.activation(product(n)[:, k - 4 * j, :], y_pad[:, k, tap:tap + SEQ],
                                                   ACT.Copy, scale=taps[:, k, tap:tap + 1])
                    ins.then_inc(S["product_ready"], 1)
            chunk_done(act, NCH - 1)
            squares_of_output(NCH - 1, 3)
            guess("post")

        @block.vector
        def _(dve):
            n_chain = [0]
            V = nc.vector

            def note(ins):
                n_chain[0] += 1
                ins.then_inc(S["dve_chain"], 1)
                return n_chain[0]

            def link(ins):
                dve.wait_ge(S["dve_chain"], note(ins))

            def split(u):
                if u >= NU or WHOLE[u]:
                    return
                n, w = SPLIT_NO[u], CHUNKS[UNITS[u][0]][2]
                dve.wait_ge(S["w_hi_ready"], n + 1)
                V.tensor_tensor(w_lo[:, n % PARTS, 0:2 * w], w_raw[:, u % RAW, 0:2 * w],
                                w_hi[:, n % PARTS, 0:2 * w].bitcast(F32), ALU.subtract)\
                    .then_inc(S["w_lo_ready"], 1)

            n_hi = [0]

            def hi_bank():
                n_hi[0] += 1
                dve.wait_ge(S["t_hi_ready"], n_hi[0])

            def lo_parts(which, k0, g, tiles=range(4), done="lo_ready", src=None):
                src = src or (lambda i: bank_pair(i // 2)[:, i % 2, :])
                for i in tiles:
                    if i % 2 == 0:
                        hi_bank()
                    ins = V.scalar_tensor_tensor(lo[which][:, k0 + i, :], src(i), g(i),
                                                 hi[which][:, k0 + i, :].bitcast(F32), ALU.mult, ALU.subtract)
                ins.then_inc(S[done], 1)

            def gated_parts(name, src, k_src, which, k0, gate_ready):
                transposed(dve, name)
                gate_ready()
                for i in range(2):
                    a = src[:, k_src + 2 * i:k_src + 2 * i + 2, :]
                    V.tensor_tensor(a, bank_pair(i), a, ALU.mult).then_inc(S["t_multiplied"], 1)
                for i in range(2):
                    hi_bank()
                    ins = V.tensor_tensor(lo[which][:, k0 + 2 * i:k0 + 2 * i + 2, :],
                                          src[:, k_src + 2 * i:k_src + 2 * i + 2, :],
                                          hi[which][:, k0 + 2 * i:k0 + 2 * i + 2, :].bitcast(F32), ALU.subtract)
                ins.then_inc(S["lo_ready"], 1)

            def variance(name, scale, wait=True):
                if wait:
                    dve.wait_ge(S["sumsq_ready"], SS_NO[name] + 1)
                V.tensor_scalar(root[name]["v"], root[name]["ss"], scale, EPS, ALU.mult, ALU.add)\
                    .then_inc(S["var_ready"], 1)

            def refine(name):
                r = root[name]
                dve.wait_ge(S["guess_ready"], RS_NO[name] + 1)
                link(V.tensor_tensor(r["t"], r["y"], r["y"], ALU.mult))
                link(V.tensor_tensor(r["t"], r["t"], r["v"], ALU.mult))
                link(V.tensor_scalar(r["t"], r["t"], -0.5, 1.5, ALU.mult, ALU.add))
                return V.tensor_tensor(r["r"], r["y"], r["t"], ALU.mult)

            def add_residual(c, name):
                chunk_done(dve, c)
                j = (c - C_OUT) % 4
                for tok in range(TT):
                    a = x_res[:, tok, j * NC:(j + 1) * NC]
                    ins = V.tensor_tensor(a, chunk_bank(c, tok), a, ALU.add)
                ins.then_inc(S[name], 1)

            def gain_of(name, k0):
                return lambda i: gain(name, k0 + i)

            def lambda_and_angles():
                dve.wait_ge(S["consts_ready"], 2)
                dve.wait_ge(S["rows_loaded"], 16 * 14)
                lam_rows = work[:, :, :].rearrange("p a b -> p (a b)")[:, 0:4 * DH]\
                    .rearrange("p (i j d) -> p i j d", i=2, j=2)
                lam_prod = probs_t[:, 0:2 * DH].rearrange("p (i d) -> p i d", i=2)
                link(V.tensor_tensor(lam_prod, lam_rows[:, :, 0, :], lam_rows[:, :, 1, :], ALU.mult))
                V.tensor_reduce(lam_sums, lam_prod, AX.X, ALU.add).then_inc(S["lam_in"], 1)
                link(V.tensor_copy(pos_f, pos_i[:, :]))
                for tok in range(TT):
                    n = note(V.tensor_scalar(rope[:, 1, tok, :], rope[:, 7, 0, :], pos_f[:, tok:tok + 1], None,
                                             ALU.mult))
                dve.wait_ge(S["dve_chain"], n)
                link(V.tensor_scalar(rope[:, 0, :, :], rope[:, 1, :, :], 1 / (2 * math.pi), ROUND,
                                     ALU.mult, ALU.add))
                link(V.tensor_scalar(rope[:, 0, :, :], rope[:, 0, :, :], ROUND, None, ALU.subtract))
                for part in (PI_A, PI_B, PI_C):
                    link(V.scalar_tensor_tensor(rope[:, 1, :, :], rope[:, 0, :, :], -part, rope[:, 1, :, :],
                                                ALU.mult, ALU.add))
                V.tensor_scalar(rope[:, 0, :, :], rope[:, 1, :, :], PI_LOW, -PI_LOW, ALU.min, ALU.max)\
                    .then_inc(S["angle_ready"], 1)

            def derived_gains():
                dve.wait_ge(S["tables_ready"], 1)
                link(V.tensor_tensor(qk_gain, gain("k_norm_g", 0), gain("b_q_norm_g", 0), ALU.mult))
                link(V.tensor_scalar(qk_gain, qk_gain, float(DH ** -0.5), None, ALU.mult))
                r_sub = ROWS["b_subln_g"][0]
                note(V.tensor_scalar(sub_gain, gains[:, r_sub:r_sub + 2], 1.0 - LAM_INIT, None, ALU.mult))

            def lambda_and_cosines():
                dve.wait_ge(S["lam_exp"], 1)
                link(V.tensor_tensor(neg_lam, lam_exps[:, 1:2], lam_exps[:, 0:1], ALU.subtract))
                note(V.tensor_scalar(neg_lam, neg_lam, -LAM_INIT, None, ALU.add))
                dve.wait_ge(S["sines_ready"], 1)
                link(V.tensor_tensor(rope[:, 3, :, :], rope[:, 3, :, :], rope[:, 3, :, :], ALU.mult))
                link(V.tensor_scalar(rope[:, 3, :, :], rope[:, 3, :, :], -2.0, 1.0, ALU.mult, ALU.add))

            def whole_parts(j):
                for k in range(4 * j, 4 * j + 4):
                    ins = V.tensor_scalar(x_t[:, k, :], bank_pair(k % 4 // 2)[:, k % 2, :],
                                          gain("a_norm_g", k), None, ALU.mult)
                ins.then_inc(S["x_whole"], 1)

            lo_parts("A", 0, gain_of("a_norm_g", 0), tiles=(0, 1), done="x_first_lo")
            split(0)
            lo_parts("A", 0, gain_of("a_norm_g", 0), tiles=(2, 3))
            split(1)
            whole_parts(0)
            sin_t, cos_t = rope[:, 2, :, :], rope[:, 3, :, :]

            r_x1, r_x2 = root["x1"]["r"], root["x2"]["r"]
            tap_done = {}
            refined = {}

            def convolve(u):
                for j, kind, tap, i in CONV_OPS[u]:
                    k = 4 * j + i
                    if kind == "first":
                        ins = V.tensor_scalar(conv[:, k, :], y_pad[:, k, 0:SEQ], taps[:, k, 0:1],
                                              gain("a_dw_b", k), ALU.mult, ALU.add)
                    elif kind == "tap":
                        dve.wait_ge(S[tap_done[k][0]], tap_done[k][1])
                        ins = V.scalar_tensor_tensor(conv[:, k, :], y_pad[:, k, tap:tap + SEQ],
                                                     taps[:, k, tap:tap + 1], conv[:, k, :],
                                                     ALU.mult, ALU.add)
                    else:
                        n = j * len(PRODUCT_TAPS) + PRODUCT_TAPS.index(tap)
                        if i == 0:
                            dve.wait_ge(S["product_ready"], n + 1)
                        name, value = tap_done[k + 1]
                        dve.wait_ge(S[name], value)
                        ins = V.tensor_tensor(conv[:, k:k + 2, :], conv[:, k:k + 2, :],
                                              product(n)[:, i:i + 2, :], ALU.add)
                    if tap == TAPS - 1 and i == 3:
                        ins.then_inc(S["conv_ready"], 1)
                    elif kind == "add" and i == 2:
                        ins.then_inc(S["product_added"], 1)
                        tap_done[k] = tap_done[k + 1] = "product_added", n + 1
                    else:
                        tap_done[k] = "dve_chain", note(ins)
                        if kind == "add":
                            tap_done[k + 1] = tap_done[k]

            def variance_of_heads(j, m):
                name = f"{m}{j}"
                dve.wait_ge(S["sumsq_ready"], SS_NO[name] + 1)
                for tok in range(TT):
                    n = note(V.tensor_reduce(root[name]["ss"][:, 4 * tok:4 * tok + 4],
                                             stage[:, j % 2, tok, :].rearrange("p (h d) -> p h d", h=4),
                                             AX.X, ALU.add))
                dve.wait_ge(S["dve_chain"], n)
                variance(name, 1.0 / DH, wait=False)

            def scale_heads(c, j, m):
                name = f"{m}{j}"
                link(refine(name))
                for tok in range(TT):
                    n = note(V.tensor_scalar(k_scale[name][:, 4 * tok:4 * tok + 4],
                                             root[name]["r"][:, 4 * tok:4 * tok + 4],
                                             r_x1[:, tok:tok + 1], None, ALU.mult))
                dve.wait_ge(S["dve_chain"], n)
                for tok in range(TT):
                    sc = k_scale[name][:, 4 * tok:4 * tok + 4].unsqueeze(2).to_broadcast([P, 4, DH])
                    ins = V.tensor_tensor(stage[:, j % 2, tok, :].rearrange("p (h d) -> p h d", h=4),
                                          chunk_bank(c, tok).rearrange("p (h d) -> p h d", h=4), sc, ALU.mult)
                ins.then_inc(S["chunk_read_dve"], 1)

            def mask_strict(a):
                a = a.rearrange("p (b n) -> p b n", n=P)[:, 0:3:2, :]
                return V.tensor_tensor(a, a, strict[:, :].unsqueeze(1).to_broadcast([P, 2, P]), ALU.mult)

            def rotate(a, heads, tmp):
                x1, x2 = a[:, :, :, 0:32], a[:, :, :, 32:64]
                shape = [P, TT, heads, 32]
                co = cos_t.unsqueeze(2).to_broadcast(shape)
                si = sin_t.unsqueeze(2).to_broadcast(shape)
                t1, t2 = tmp
                note(V.tensor_tensor(t1, x1, si, ALU.mult))
                link(V.tensor_tensor(t2, x2, si, ALU.mult))
                note(V.tensor_tensor(x1, x1, co, ALU.mult))
                link(V.tensor_tensor(x2, x2, co, ALU.mult))
                note(V.tensor_tensor(x1, x1, t2, ALU.subtract))
                return V.tensor_tensor(x2, x2, t1, ALU.add)

            for u, (c, s) in enumerate(UNITS):
                h, b = divmod(u - DIFF_FROM, DIFF_STEP)
                if 0 <= h < HEADS:
                    if b == 0:
                        dve.wait_ge(S["d_scores"], h + 1)
                        V.reduce_max(neg_max[:, 0:4:2], PS[:, 6:8, 0:128], AX.X, negate=True)
                        V.reduce_max(neg_max[:, 1:4:2], PS[:, 6:8, 128:384], AX.X, negate=True)\
                            .then_inc(S["d_negmax"], 1)
                    if b == 2:
                        dve.wait_ge(S["d_exp"], h + 1)
                        link(V.reciprocal(recips, sums))
                        link(V.tensor_scalar(neg_r, recips[:, 2:4], neg_lam, None, ALU.mult))
                        for tok, (f, e) in enumerate(((0, 128), (128, 384))):
                            n = note(V.tensor_scalar(work[:, 1, f:e], work[:, 1, f:e], neg_r[:, tok:tok + 1],
                                                     None, ALU.mult))
                        dve.wait_ge(S["dve_chain"], n)
                        for tok, (f, e) in enumerate(((0, 128), (128, 384))):
                            ins = V.scalar_tensor_tensor(work[:, 0, f:e], work[:, 0, f:e],
                                                         recips[:, tok:tok + 1], work[:, 1, f:e],
                                                         ALU.mult, ALU.add)
                        ins.then_inc(S["d_probs"], 1)
                    if b == 4:
                        dve.wait_ge(S["d_out"], h + 1)
                        V.tensor_copy(heads_out[:, h % 4, :, :],
                                      PS[:, 7, :].rearrange("p (t n) -> p t n", t=TT))\
                            .then_inc(S["on_ready"], 1)
                h, b = divmod(u - MLA_FROM, MLA_STEP)
                if 0 <= h < HEADS:
                    if b == 0:
                        dve.wait_ge(S["m_scores"], h + 1)
                        V.reduce_max(neg_max[:, 0:1], PS[:, 6, 0:128], AX.X, negate=True)
                        V.reduce_max(neg_max[:, 1:2], PS[:, 6, 128:384], AX.X, negate=True)\
                            .then_inc(S["m_negmax"], 1)
                    if b == 1:
                        m = h % 2
                        dve.wait_ge(S["m_exp"], h + 1)
                        link(V.reciprocal(recips[:, 0:2], sums[:, 0:2]))
                        for tok, (f, e) in enumerate(((0, 128), (128, 384))):
                            ins = V.tensor_scalar(work[:, m, f:e], work[:, m, f:e], recips[:, tok:tok + 1],
                                                  None, ALU.mult)
                        ins.then_inc(S["m_probs"], 1)
                h, b = divmod(u - SB_FROM, SB_STEP)
                if 0 <= h < HEADS:
                    z = PS[:, 6, 0:384]
                    if b == 1:
                        dve.wait_ge(S["s_soft"], h + 1)
                        link(V.scalar_tensor_tensor(work[:, 1, :], z, 0.0, work[:, 0, :], ALU.max, ALU.add))
                        link(V.tensor_tensor(probs_t[:, :], z, work[:, 1, :], ALU.subtract))
                        mask_strict(work[:, 1, :]).then_inc(S["s_keep"], 1)
                split(u + AHEAD)
                if u in X_AT:
                    lo_parts("A", 4 * X_AT.index(u), gain_of("a_norm_g", 4 * X_AT.index(u)))
                if u == 6:
                    dve.wait_ge(S["x_squared"], 2)
                    variance("x", 1.0 / D, wait=False)
                    refine("x").then_inc(S["x_scale_ready"], 1)
                if u == 8:
                    lambda_and_angles()
                if u == 9:
                    derived_gains()
                if u == 11:
                    lambda_and_cosines()
                if s == 0 and 2 <= c <= C_Z and c % 2 == 0:
                    j = c // 2 - 1
                    dve.wait_ge(S["sig_ready"], j + 1)
                    V.tensor_tensor(stage[:, 1, :, :], stage[:, 0, :, :], stage[:, 1, :, :], ALU.mult)\
                        .then_inc(S["y_ready"], 1)
                for j, f in enumerate(CONV_FROM):
                    if f <= u < f + CONV_SLOTS:
                        if u == f:
                            dve.wait_ge(S["t_copied"], COPY_NO[f"y{j}"] + 1)
                        convolve(u)
                    if u == STATS_AT[j]:
                        for tok in range(TT):
                            dve.wait_ge(S["stats_full"], 2 * j + tok + 1)
                            g = 4 * tok + j
                            ins = V.bn_stats(bn[:, 6 * g:6 * g + 6], PS[:, 6 + tok, :])
                            ins.then_inc(S["stats_read"], 1)
                if u == MOMENTS_AT:
                    dve.wait_ge(S["stats_read"], 8)
                    for tok in range(TT):
                        n = note(V.bn_aggr(mv[:, 2 * tok:2 * tok + 2], bn[:, 24 * tok:24 * tok + 24]))
                    dve.wait_ge(S["dve_chain"], n)
                    V.tensor_scalar(root["ln"]["v"], mv[:, 1:4:2], 1.0, EPS, ALU.mult, ALU.add)\
                        .then_inc(S["var_ready"], 1)
                    link(refine("ln"))
                    for tok in range(TT):
                        V.tensor_scalar(diag[:, tok, :], ident[:, :], mv[:, 2 * tok:2 * tok + 1], None, ALU.mult)
                        ins = V.tensor_scalar(diag[:, 2 + tok, :], ident[:, :],
                                              root["ln"]["r"][:, tok:tok + 1], None, ALU.mult)
                    ins.then_inc(S["diag_ready"], 1)
                if u in NORM_AT:
                    dve.wait_ge(S["moments_ready"], 1)
                    j = NORM_AT.index(u)
                    a = conv[:, 4 * j:4 * j + 4, :]
                    link(V.tensor_tensor(a, a, moments[:, 0:1, :].to_broadcast([P, 4, SEQ]), ALU.subtract))
                    V.tensor_tensor(a, a, moments[:, 1:2, :].to_broadcast([P, 4, SEQ]), ALU.mult)\
                        .then_inc(S["normed"], 1)
                if u in Z_AT:
                    j = Z_AT.index(u)
                    gated_parts(f"z{j}", conv, 4 * j, "B", 4 * j,
                                lambda: dve.wait_ge(S["silu_ready"], j + 1))
                if s == 0 and C_OUT < c <= C_K:
                    add_residual(c - 1, "x1_ready")
                if s == 2 and C_OUT < c <= C_K:
                    lo_parts("A", 4 * (c - C_OUT - 1), gain_of("kv_norm_g", 4 * (c - C_OUT - 1)))
                if u == FIRST[C_K] + 6:
                    variance("x1", 1.0 / D)
                    refine("x1").then_inc(S["x1_scale_ready"], 1)
                if s == 4 and C_K <= c < C_V:
                    dve.wait_ge(S["x1_kept"], c - C_K + 1)
                    lo_parts("B", 4 * (c - C_K), gain_of("b_norm_g", 4 * (c - C_K)),
                             src=lambda i: x1_t[:, 4 * (c - C_K) + i, :])
                for m, c0 in (("k", C_K), ("q", C_Q)):
                    if s == 0 and c0 < c <= c0 + 4:
                        variance_of_heads(c - c0 - 1, m)
                    if s == 1 and c0 < c <= c0 + 4:
                        scale_heads(c - 1, c - c0 - 1, m)
                h, b = divmod(u - DIFF_FROM - DIFF_STEP, DIFF_STEP)
                if 0 <= h < HEADS and b == 0:
                    variance(f"o{h}", 1.0 / (2 * DH))
                if 0 <= h < HEADS and b == 2:
                    refined[h] = note(refine(f"o{h}"))
                if u in GATE_AT:
                    j = GATE_AT.index(u)
                    dve.wait_ge(S["chunk_read_act"], acts_up_to(C_ZB + j))
                    dve.wait_ge(S["dve_chain"], refined[2 * j + 1])
                    for h in (2 * j, 2 * j + 1):
                        for tok in range(TT):
                            a = heads_out[:, h % 4, tok, :]
                            ins = V.scalar_tensor_tensor(
                                a, a, root[f"o{h}"]["r"][:, tok:tok + 1],
                                stage[:, j % 2, tok, 256 * (h % 2):256 * (h % 2) + 256], ALU.mult, ALU.mult)
                    ins.then_inc(S["d_gated"], 1)
                if u in OG_AT:
                    lo_parts("A", 4 * OG_AT.index(u), lambda i: sub_gain[:, i % 2:i % 2 + 1])
                if s == 0 and C_OUTB < c <= C_CQ:
                    add_residual(c - 1, "x2_ready")
                if s == 2 and C_OUTB < c <= C_CQ:
                    lo_parts("B", 4 * (c - C_OUTB - 1), gain_of("pre_norm_w_2", 4 * (c - C_OUTB - 1)))
                if u == FIRST[C_CQ] + 6:
                    variance("x2", 1.0 / D)
                    refine("x2").then_inc(S["x2_scale_ready"], 1)
                if u == FIRST[C_CKV]:
                    variance("cq", 1.0 / 512)
                if u == FIRST[C_CKV] + 1:
                    link(refine("cq"))
                    V.tensor_tensor(cq_scale, root["cq"]["r"], r_x2, ALU.mult).then_inc(S["cq_scaled"], 1)
                if u == FIRST[C_CKV] + 4:
                    lo_parts("A", 0, gain_of("q_norm_w_2", 0))
                if u == FIRST[C_QUP]:
                    variance("ckv", 1.0 / 256)
                    dve.wait_ge(S["kr_staged"], 1)
                    rotate(stage[:, 1, :, 256:320].unsqueeze(2), 1,
                           (rope[:, 4, :, :].unsqueeze(2), rope[:, 5, :, :].unsqueeze(2)))\
                        .then_inc(S["kr_roped"], 1)
                if u == FIRST[C_QUP] + 1:
                    link(refine("ckv"))
                    V.tensor_tensor(ckv_scale, root["ckv"]["r"], r_x2, ALU.mult).then_inc(S["ckv_scaled"], 1)
                if u == FIRST[C_QUP] + 2:
                    lo_parts("A", 4, gain_of("kv_norm_w_2", 0), tiles=range(2))
                if s == 0 and C_QUP < c <= C_KVUP:
                    j = c - C_QUP - 1
                    dve.wait_ge(S["chunk_read_act"], acts_up_to(c - 1))
                    tmp = [rope[:, i, :, :] for i in (4, 5, 0, 1)]
                    for h in range(2):
                        a = qu_stage[:, j % 2, :, h * 192 + DH:h * 192 + DH + ROT].unsqueeze(2)
                        ins = rotate(a, 1, (tmp[2 * h].unsqueeze(2), tmp[2 * h + 1].unsqueeze(2)))
                        if h == 0:
                            note(ins)
                    ins.then_inc(S["qu_roped"], 1)
                for m, c0, k0 in (("mg", C_MG, 8), ("sg", C_SG, 0)):
                    if u in HG_AT[m]:
                        j = HG_AT[m].index(u)
                        src, done = (qn_t, "m_out_copied") if m == "mg" else (sq_t, "s_out_copied")
                        gated_parts(f"{m}{j}", src, 4 * j, "A", k0 + 4 * j,
                                    lambda: dve.wait_ge(S[done], 4 * j + 4))
                h, b = divmod(u - SB_FROM, SB_STEP)
                if 0 <= h < HEADS:
                    if b == 2:
                        dve.wait_ge(S["s_later"], h + 1)
                        V.tensor_tensor(probs_t[:, :], PS[:, 7, 0:384], probs_t[:, :], ALU.add)\
                            .then_inc(S["s_logit"], 1)
                    if b == 3:
                        dve.wait_ge(S["s_weight"], h + 1)
                        mask_strict(sb_weight(h)).then_inc(S["s_masked"], 1)
                if s == 0 and c > C_OUT2:
                    scale_output(nc, S, dve, c - 1, c - C_OUT2 - 1, chunk_bank, yw, post_gain)
                if u in X_AT:
                    whole_parts(X_AT.index(u))
            chunk_done(dve, NCH - 1)
            for tok in (1, 0):
                if tok == 0:
                    dve.wait_ge(S["y_squared"], 7)
                V.tensor_tensor(yw[:, tok, 3 * NC:4 * NC], chunk_bank(NCH - 1, tok),
                                post_gain[:, 3 * NC:4 * NC], ALU.mult).then_inc(S["last_scaled"], 1)
            dve.wait_ge(S["y_squared"], 8)
            link(V.tensor_reduce(root["post"]["ss"], y_sums.rearrange("p (t j) -> p t j", t=TT), AX.X, ALU.add))
            variance("post", 1.0 / D, wait=False)
            link(refine("post"))
            for j in range(4):
                if j == 3:
                    dve.wait_ge(S["last_scaled"], 2)
                for tok in range(TT):
                    a = yw[:, tok, j * NC:(j + 1) * NC]
                    V.scalar_tensor_tensor(a, a, root["post"]["r"][:, tok:tok + 1],
                                           x_res[:, tok, j * NC:(j + 1) * NC], ALU.mult, ALU.add)\
                        .then_inc(S["final_ready"], 1)

        @block.tensor
        def _(pe):
            T = nc.tensor

            def t_free(name):
                n = T_NO[name]
                if n == 0:
                    return
                prev, kind = T_EVENTS[n - 1]
                if kind == "copy":
                    pe.wait_ge(S["t_copied"], COPY_NO[prev] + 1)
                elif kind == "whole":
                    pe.wait_ge(S["x_whole"], int(prev[1]) + 1)
                elif kind == "mul":
                    pe.wait_ge(S["t_multiplied"], 2 * MUL_NO[prev] + 2)
                else:
                    pe.wait_ge(S["lo_ready"], LO_NO[prev] + 1)

            def transpose_chunk(name, src, n=4):
                t_free(name)
                for i in range(n):
                    for tok in range(TT):
                        at = (i % 2) * SEQ + tok * P
                        ins = T.transpose(PS[:, 4 + i // 2, at:at + P], src(tok, i), ident[:, :])
                ins.then_inc(S["t_full"], 1)

            pieces = [(0, 0, 0, True), (P, P, 0, False), (2 * P, P, P, True)]

            def masked_scores(bank, operands):
                for f, q0, k0, masked in pieces:
                    for i, (q, k) in enumerate(operands):
                        ins = T.matmul(PS[:, bank, f:f + P], q[:, q0:q0 + P], k[:, k0:k0 + P],
                                       start=i == 0, stop=not masked and i == len(operands) - 1)
                    if masked:
                        ins = T.matmul(PS[:, bank, f:f + P], mask_row[0:1, 0:P], mask_row[0:1, P:2 * P],
                                       start=False, stop=True)
                return ins

            def staged(buf):
                return lambda tok, i: stage[:, buf, tok, i * P:(i + 1) * P]

            def rows(j):
                return lambda tok, i: x_res[:, tok, j * NC + i * P:j * NC + (i + 1) * P]

            source = {}
            for c in range(NCH):
                for k in range(KT):
                    g = k // 4
                    if c < C_OUT:
                        source[c, k] = f"x{g}"
                    elif c < C_K:
                        source[c, k] = f"z{g}"
                    elif c < C_Q:
                        source[c, k] = f"w{g}"
                    elif c < C_OUTB:
                        source[c, k] = f"b{g}"
                    elif c < C_CQ:
                        source[c, k] = f"og{g}"
                    elif C_QUP <= c < C_KVUP:
                        source[c, k] = "cq"
                    elif C_KVUP <= c < C_SBQ:
                        source[c, k] = "ckv"
                    elif c >= C_OUT2:
                        source[c, k] = f"sg{g}" if g < 2 else f"mg{g - 2}"
                    else:
                        source[c, k] = f"v{g}"

            def products(u):
                c, i = UNITS[u]
                _, _, w, kts, which, k_first = CHUNKS[c]
                if i == 0 and c >= 2:
                    if c - 2 in BY_DVE:
                        name, n = dve_reads(c - 2)
                        pe.wait_ge(S[name], n)
                    else:
                        pe.wait_ge(S["chunk_read_act" if c - 2 not in B_CHUNKS else "y_ready"],
                                   acts_up_to(c - 2) if c - 2 not in B_CHUNKS else (c - 1) // 2)
                if u == 0:
                    pe.wait_ge(S["x_first_lo"], 1)
                else:
                    pe.wait_ge(S["lo_ready"], LO_NO[source[c, kts[2 * i + 1]]] + 1)
                first, last = i == 0, i == len(kts) // 2 - 1
                if WHOLE[u]:
                    pe.wait_ge(S[f"w{u % RAW}_loaded"], 16 * (u // RAW + 1))
                    pe.wait_ge(S["x_whole"], 4)
                    raw = w_view(w_raw, u % RAW, w)
                    for kk in range(2):
                        k = k_first + kts[2 * i + kk]
                        for tok in range(TT):
                            ins = T.matmul(chunk_bank(c, tok), x_t[:, k, tok * P:(tok + 1) * P],
                                           raw[:, kk, :], start=first and kk == 0, stop=last and kk == 1)
                else:
                    n = SPLIT_NO[u]
                    pe.wait_ge(S["w_lo_ready"], n + 1)
                    wh, wl = w_view(w_hi, n % PARTS, w), w_view(w_lo, n % PARTS, w)
                    for kk in range(2):
                        k = k_first + kts[2 * i + kk]
                        for tok in range(TT):
                            ah = hi[which][:, k, tok * P:(tok + 1) * P]
                            al = lo[which][:, k, tok * P:(tok + 1) * P]
                            bank = chunk_bank(c, tok)
                            T.matmul(bank, ah, wh[:, kk, :], start=first and kk == 0, stop=False)
                            T.matmul(bank, ah, wl[:, kk, :], start=False, stop=False)
                            ins = T.matmul(bank, al, wh[:, kk, :], start=False, stop=last and kk == 1)
                ins.then_inc(S["units_done"], 1)

            pe.wait_ge(S["consts_ready"], 2)
            pe.wait_ge(S["gain_loaded"], 16)
            T.transpose(PS[:, 6, 0:KT], stage[0:KT, 0, 0, 0:P], ident[0:KT, 0:KT]).then_inc(S["gain_full"], 1)
            pe.wait_ge(S["x0_loaded"], 16)
            transpose_chunk("x0", rows(0))

            for u, (c, s) in enumerate(UNITS):
                if u in X_AT:
                    j = X_AT.index(u)
                    pe.wait_ge(S[f"x{j}_loaded"], 16)
                    transpose_chunk(f"x{j}", rows(j))
                if u == 4:
                    pe.wait_ge(S["rows_loaded"], 16 * 14)
                    pe.wait_ge(S["gain_ready"], 1)
                    T.transpose(PS[:, 6, 0:NROWS], stage[0:NROWS, 0, 0, 0:P], ident[0:NROWS, 0:NROWS])
                    for k in range(KT):
                        ins = T.transpose(PS[:, 7, k * TAPS:(k + 1) * TAPS], junk[0:TAPS, k * P:(k + 1) * P],
                                          ident[0:TAPS, 0:TAPS])
                    ins.then_inc(S["tables_full"], 1)
                if s == 3 and 2 <= c <= C_Z and c % 2 == 0:
                    j = c // 2 - 1
                    pe.wait_ge(S["y_ready"], j + 1)
                    transpose_chunk(f"y{j}", staged(1))
                for j, f in enumerate(CONV_FROM):
                    if u == STATS_AT[j]:
                        pe.wait_ge(S["conv_ready"], j + 1)
                        if j:
                            pe.wait_ge(S["stats_read"], 2 * j)
                        else:
                            pe.wait_ge(S["tables_ready"], 1)
                        for tok in range(TT):
                            for i in range(4):
                                ins = T.transpose(PS[:, 6 + tok, i * P:(i + 1) * P],
                                                  conv[:, 4 * j + i, tok * P:(tok + 1) * P], ident[:, :])
                            ins.then_inc(S["stats_full"], 1)
                if u == MOMENTS_AT + 2:
                    pe.wait_ge(S["diag_ready"], 1)
                    for i in range(4):
                        ins = T.matmul(PS[:, 6, i * P:(i + 1) * P], ones[:, :], diag[:, i, :],
                                       start=True, stop=True)
                    ins.then_inc(S["moments_full"], 1)
                if u in Z_AT:
                    j = Z_AT.index(u)
                    pe.wait_ge(S["chunk_read_act"], acts_up_to(C_Z + j))
                    transpose_chunk(f"z{j}", staged(j % 2))
                if s == 2 and C_OUT < c <= C_K:
                    j = c - C_OUT - 1
                    pe.wait_ge(S["x1_ready"], j + 1)
                    transpose_chunk(f"w{j}", rows(j))
                for m, c0 in (("k", C_K), ("q", C_Q)):
                    if s == 3 and c0 < c <= c0 + 4:
                        j = c - c0 - 1
                        pe.wait_ge(S["chunk_read_dve"], j + 1 + (4 if m == "q" else 0))
                        transpose_chunk(f"{m}{j}", staged(j % 2))
                h, b = divmod(u - DIFF_FROM, DIFF_STEP)
                if 0 <= h < HEADS:
                    if b == 0:
                        pe.wait_ge(S["t_copied"], COPY_NO[f"q{h // 2}"] + 1)
                        if h:
                            pe.wait_ge(S["on_ready"], h)
                        for m in range(2):
                            ins = masked_scores(6 + m, [(q_t[:, 2 * h + m, :], k_t[:, 2 * h + m, :])])
                        ins.then_inc(S["d_scores"], 1)
                    if b == 3:
                        pe.wait_ge(S["d_probs"], h + 1)
                        for i in range(3):
                            ins = T.transpose(PS[:, 6, i * P:(i + 1) * P], work[:, 0, i * P:(i + 1) * P],
                                              ident[:, :])
                        ins.then_inc(S["d_pt"], 1)
                    if b == 4:
                        pe.wait_ge(S["d_pt_copied"], h + 1)
                        v0, v1 = (vals[:, i, 256 * h:256 * h + 256] for i in range(2))
                        T.matmul(PS[:, 7, 0:256], probs_t[:, 0:P], v0, start=True, stop=True)
                        T.matmul(PS[:, 7, 256:512], probs_t[:, P:2 * P], v0, start=True, stop=False)
                        T.matmul(PS[:, 7, 256:512], probs_t[:, 2 * P:3 * P], v1, start=False, stop=True)\
                            .then_inc(S["d_out"], 1)
                if u in OG_AT:
                    j = OG_AT.index(u)
                    pe.wait_ge(S["d_gated"], j + 1)
                    transpose_chunk(f"og{j}", lambda tok, i: heads_out[:, (2 * j + i // 2) % 4, tok,
                                                                       (i % 2) * P:(i % 2 + 1) * P])
                if s == 2 and C_OUTB < c <= C_CQ:
                    j = c - C_OUTB - 1
                    pe.wait_ge(S["x2_ready"], j + 1)
                    transpose_chunk(f"v{j}", rows(j))
                if u == FIRST[C_CKV] + 4:
                    pe.wait_ge(S["chunk_read_act"], acts_up_to(C_CQ))
                    transpose_chunk("cq", staged(0))
                if u == FIRST[C_QUP] + 2:
                    pe.wait_ge(S["chunk_read_act"], acts_up_to(C_CKV))
                    pe.wait_ge(S["kr_roped"], 1)
                    t_free("ckv")
                    for tok in range(TT):
                        T.transpose(PS[0:ROT, 5, tok * P:(tok + 1) * P], stage[:, 1, tok, 256:320], ident[:, :])
                    for i in range(2):
                        for tok in range(TT):
                            at = i * SEQ + tok * P
                            ins = T.transpose(PS[:, 4, at:at + P], stage[:, 1, tok, i * P:(i + 1) * P],
                                              ident[:, :])
                    ins.then_inc(S["t_full"], 1)
                for j in range(4):
                    if u == QU_AT[j]:
                        pe.wait_ge(S["qu_roped"], j + 1)
                        t_free(f"qu{j}")
                        for h in range(2):
                            for tok in range(TT):
                                at = h * SEQ + tok * P
                                T.transpose(PS[:, 4, at:at + P],
                                            qu_stage[:, j % 2, tok, h * 192:h * 192 + P], ident[:, :])
                                ins = T.transpose(PS[0:ROT, 5, at:at + P],
                                                  qu_stage[:, j % 2, tok, h * 192 + P:h * 192 + 192],
                                                  ident[:, :])
                        ins.then_inc(S["t_full"], 1)
                    if u == FIRST[C_KVUP + j + 1] + 1:
                        pe.wait_ge(S["chunk_read_act"], acts_up_to(C_KVUP + j))
                        transpose_chunk(f"ku{j}", staged(j % 2), n=2)
                for m, c0 in (("sq", C_SBQ), ("sk", C_SBK)):
                    if s == 2 and c0 < c <= c0 + 2:
                        j = c - c0 - 1
                        pe.wait_ge(S["chunk_read_act"], acts_up_to(c - 1))
                        transpose_chunk(f"{m}{j}", staged(j))
                for m, c0 in (("mg", C_MG), ("sg", C_SG)):
                    if u in HG_AT[m]:
                        j = HG_AT[m].index(u)
                        pe.wait_ge(S["chunk_read_act"], acts_up_to(c0 + j))
                        transpose_chunk(f"{m}{j}", staged(j))
                h, b = divmod(u - MLA_FROM, MLA_STEP)
                if 0 <= h < HEADS:
                    if b == 0:
                        if h:
                            pe.wait_ge(S["m_out_copied"], h)
                        else:
                            pe.wait_ge(S["t_copied"], COPY_NO["ku3"] + 1)
                        ins = masked_scores(6, [(qn_t[:, h, :], kn_t[:, h, :]),
                                                (qr_t[0:ROT, h, :], kr_t[0:ROT, :])])
                        ins.then_inc(S["m_scores"], 1)
                    if b == 2:
                        pe.wait_ge(S["m_probs"], h + 1)
                        for i in range(3):
                            ins = T.transpose(PS[:, 7, i * P:(i + 1) * P], work[:, h % 2, i * P:(i + 1) * P],
                                              ident[:, :])
                        ins.then_inc(S["m_pt"], 1)
                    if b == 3:
                        pe.wait_ge(S["m_pt_copied"], h + 1)
                        T.matmul(PS[:, 6, 0:SEQ], v_mla[:, 0, h * DH:(h + 1) * DH], probs_t[:, 0:SEQ],
                                 start=True, stop=False)
                        T.matmul(PS[:, 6, P:SEQ], v_mla[:, 1, h * DH:(h + 1) * DH], probs_t[:, SEQ:384],
                                 start=False, stop=True).then_inc(S["m_out"], 1)
                h, b = divmod(u - SB_FROM, SB_STEP)
                if 0 <= h < HEADS:
                    if b == 0:
                        if h:
                            pe.wait_ge(S["s_keep"], h)
                        else:
                            pe.wait_ge(S["m_out_copied"], HEADS)
                        T.matmul(PS[:, 6, 0:SEQ], sk_t[:, h, 0:P], sq_t[:, h, :], start=True, stop=True)
                        T.matmul(PS[:, 6, SEQ:384], sk_t[:, h, P:SEQ], sq_t[:, h, P:SEQ], start=True, stop=True)\
                            .then_inc(S["s_scores"], 1)
                    if b == 2:
                        pe.wait_ge(S["s_keep"], h + 1)
                        if h:
                            pe.wait_ge(S["s_out_copied"], h)
                        T.matmul(PS[:, 7, 0:SEQ], after[:, :], work[:, 1, 0:SEQ], start=True, stop=False)
                        T.matmul(PS[:, 7, P:SEQ], neg_ones[:, :], work[:, 1, SEQ:384], start=False, stop=True)
                        T.matmul(PS[:, 7, SEQ:384], after[:, :], work[:, 1, SEQ:384], start=True, stop=True)\
                            .then_inc(S["s_later"], 1)
                h, b = divmod(u - SB_FROM - SB_STEP, SB_STEP)
                if 0 <= h < HEADS and b == 1:
                    pe.wait_ge(S["s_masked"], h + 1)
                    pe.wait_ge(S["chunk_read_act"], acts_up_to(C_SBV + 1))
                    w = sb_weight(h)
                    T.matmul(PS[:, 7, 0:SEQ], v_sb[:, 0, h * DH:(h + 1) * DH], w[:, 0:SEQ],
                             start=True, stop=False)
                    T.matmul(PS[:, 7, P:SEQ], v_sb[:, 1, h * DH:(h + 1) * DH], w[:, SEQ:384],
                             start=False, stop=True).then_inc(S["s_out"], 1)
                products(u)


B_CHUNKS = {1, 3, 5, 7}


def acts_up_to(c):
    return sum(1 for n in range(c + 1) if n not in BY_DVE and n not in B_CHUNKS)


def dve_reads(c):
    if C_OUT <= c < C_K:
        return "x1_ready", c - C_OUT + 1
    if C_OUTB <= c < C_CQ:
        return "x2_ready", c - C_OUTB + 1
    if c >= C_OUT2:
        return "y_scaled", c - C_OUT2 + 1
    return "chunk_read_dve", c - C_K + 1 if c < C_V else c - C_Q + 5


def scale_output(nc, S, dve, c, j, chunk_bank, yw, post_gain):
    if j == 0:
        dve.wait_ge(S["post_gain_loaded"], 16)
    for tok in range(TT):
        dve.wait_ge(S["y_squared"], 2 * j + tok + 1)
        ins = nc.vector.tensor_tensor(yw[:, tok, j * NC:(j + 1) * NC], chunk_bank(c, tok),
                                      post_gain[:, j * NC:(j + 1) * NC], ALU.mult)
    ins.then_inc(S["y_scaled"], 1)


_INS = ["x", "a_norm_g", "a_w_in", "a_dw_w", "a_dw_b", "a_ln_g", "a_ln_b", "a_w_out", "kv_norm_g", "w_kv",
        "k_norm_g", "b_norm_g", "b_w_in", "b_q_norm_g", "b_lambda", "b_subln_g", "b_w_out", "positions_2",
        "pre_norm_w_2", "w_in_2", "q_norm_w_2", "w_q_up_2", "kv_norm_w_2", "w_kv_up_2", "w_out_2",
        "post_norm_w_2"]


def kernel(**inputs):
    import numpy as _np
    import concourse.bacc as _bacc
    from concourse import mybir as _mybir
    from concourse.bass_utils import run_bass_kernel_spmd as _run

    nc = _bacc.Bacc("TRN2", target_bir_lowering=False, num_devices=1)
    arrays, tensors = {}, {}
    for name in _INS:
        a = _np.ascontiguousarray(inputs[name])
        if name == "w_kv":
            a = a.reshape(1, *a.shape)
        arrays[f"in_{name}"] = a
        tensors[name] = nc.dram_tensor(f"in_{name}", a.shape, _mybir.dt.from_np(a.dtype),
                                       kind="ExternalInput").ap()
    out = nc.dram_tensor("out_y", (1, SEQ, D), _mybir.dt.float32, kind="ExternalOutput").ap()
    hybrid_program(nc, tensors, out)
    r = _run(nc, [arrays], core_ids=[0])
    return r.results[0]["out_y"]
```
